# Optimizing a Trainium2 kernel written in Bass

```python
import jax
import jax.numpy as jnp
from jax import lax
import numpy as np

D_MODEL = 2048
BATCH = 1
SEQ = 512
DEPTH = 1

SB_HEADS = 16
SB_HEAD_DIM = 64
SB_WIDTH = SB_HEADS * SB_HEAD_DIM
SB_BLOCK = 128
RWKV_HEADS = 16
RWKV_HEAD_DIM = 64
RWKV_WIDTH = RWKV_HEADS * RWKV_HEAD_DIM
DECAY_LORA = 64
ICLR_LORA = 64
GATE_LORA = 160
N_SHIFT_MIX = 6
GN_EPS = 64e-5
IN_COLS = 3 * SB_WIDTH + 4 * RWKV_WIDTH + 2 * D_MODEL
IN_SPLITS = (SB_WIDTH, 2 * SB_WIDTH, 3 * SB_WIDTH,
             3 * SB_WIDTH + RWKV_WIDTH, 3 * SB_WIDTH + 2 * RWKV_WIDTH,
             3 * SB_WIDTH + 3 * RWKV_WIDTH, 3 * SB_WIDTH + 4 * RWKV_WIDTH,
             3 * SB_WIDTH + 4 * RWKV_WIDTH + D_MODEL)
PEER_HEADS = 8
PEER_TOPK = 16
N_KEYS = 128
N_EXPERTS = N_KEYS * N_KEYS
PEER_KEY_DIM = 256
PEER_CHUNK = 128
PLE_DIM = 256
LN_EPS = 1e-5
DEEPNORM_ALPHA = (2 * DEPTH) ** 0.25
DEEPNORM_BETA = (8 * DEPTH) ** -0.25

kernel_name = 'hybrid_stickbreak_rwkv7_peer_block'

def _layer_norm(x, g, b):
    xf = x.astype(jnp.float32)
    mu = jnp.mean(xf, axis=-1, keepdims=True)
    var = jnp.mean(jnp.square(xf - mu), axis=-1, keepdims=True)
    return ((xf - mu) * lax.rsqrt(var + LN_EPS) * g + b).astype(x.dtype)

def _shift_lerp(z, mu):
    prev = jnp.pad(z, ((0, 0), (1, 0), (0, 0)))[:, :-1]
    return z + (prev - z) * mu

def _stick_breaking_attention(q, k, v):
    b, t, h, dh = q.shape
    n_blocks = t // SB_BLOCK
    scale = dh ** -0.5
    q_blocks = q.reshape(b, n_blocks, SB_BLOCK, h, dh).transpose(1, 0, 3, 2, 4)
    k_t = k.transpose(0, 2, 1, 3)
    v_t = v.transpose(0, 2, 1, 3)
    key_pos = jnp.arange(t)
    starts = jnp.arange(n_blocks) * SB_BLOCK

    def block(args):
        q_blk, start = args
        z = jnp.einsum('bhqd,bhkd->bhqk', q_blk, k_t).astype(jnp.float32) * scale
        q_pos = start + jnp.arange(SB_BLOCK)
        causal = key_pos[None, :] < q_pos[:, None]
        log_keep = jnp.where(causal, jax.nn.log_sigmoid(-z), 0.0)
        log_later = lax.cumsum(log_keep, axis=3, reverse=True) - log_keep
        w = jnp.where(causal, jnp.exp(jax.nn.log_sigmoid(z) + log_later), 0.0)
        return jnp.einsum('bhqk,bhkd->bhqd', w.astype(v_t.dtype), v_t)

    out = lax.map(block, (q_blocks, starts))
    return out.transpose(1, 0, 3, 2, 4).reshape(b, t, h * dh)

def _rwkv7_scan(r, log_w, k, v, a_vec, b_vec):
    bsz, _, h, n = r.shape

    def step(state, inp):
        r_t, lw_t, k_t, v_t, a_t, b_t = inp
        sa = jnp.einsum('bhvk,bhk->bhv', state, a_t)
        state = (state * jnp.exp(lw_t)[:, :, None, :]
                 + sa[..., None] * b_t[:, :, None, :]
                 + v_t[..., None] * k_t[:, :, None, :])
        return state, jnp.einsum('bhvk,bhk->bhv', state, r_t)

    xs = tuple(z.astype(jnp.float32).transpose(1, 0, 2, 3) for z in (r, log_w, k, v, a_vec, b_vec))
    _, y = lax.scan(step, jnp.zeros((bsz, h, n, n), jnp.float32), xs)
    return y.transpose(1, 0, 2, 3)

def _rwkv7_time_mix(r_in, k_in, v_in, c_in, mu, w0, w_lora1, w_lora2, a0, a_lora1, a_lora2,
                    g_lora1, g_lora2, k_k, k_a, r_k, lnx_w, lnx_b):
    bsz, t, _ = r_in.shape

    def heads(z):
        return z.reshape(bsz, t, RWKV_HEADS, RWKV_HEAD_DIM)

    r = _shift_lerp(r_in, mu[0])
    k = _shift_lerp(k_in, mu[1])
    v = _shift_lerp(v_in, mu[2])
    xw = _shift_lerp(c_in, mu[3])
    xa = _shift_lerp(c_in, mu[4])
    xg = _shift_lerp(c_in, mu[5])
    w = -jax.nn.softplus(-(w0 + jnp.tanh(xw @ w_lora1) @ w_lora2)) - 0.5
    log_decay = -jnp.exp(w.astype(jnp.float32))
    a = jax.nn.sigmoid(a0 + (xa @ a_lora1) @ a_lora2)
    g = jax.nn.sigmoid(xg @ g_lora1) @ g_lora2
    kk = heads(k * k_k).astype(jnp.float32)
    kk = kk / jnp.maximum(jnp.sqrt(jnp.sum(kk * kk, axis=-1, keepdims=True)), 1e-12)
    k = k * (1.0 + (a - 1.0) * k_a)
    rh, kh, vh, ah = heads(r), heads(k), heads(v), heads(a)
    y = _rwkv7_scan(rh, heads(log_decay), kh, vh, -kk, kk * ah)
    mean = jnp.mean(y, axis=-1, keepdims=True)
    var = jnp.mean(jnp.square(y - mean), axis=-1, keepdims=True)
    y = ((y - mean) * lax.rsqrt(var + GN_EPS)).reshape(bsz, t, RWKV_WIDTH) * lnx_w + lnx_b
    bonus = jnp.sum(rh * kh * r_k, axis=-1, keepdims=True) * vh
    y = y.astype(r_in.dtype) + bonus.reshape(bsz, t, RWKV_WIDTH)
    return y * g

def _peer_ffn(x, w_q, sub_keys, expert_u, expert_v):
    bsz, t, d = x.shape
    q = (x @ w_q).reshape(bsz, t, PEER_HEADS, 2, PEER_KEY_DIM // 2)
    s = jnp.einsum('bthcd,cnd->bthcn', q, sub_keys).astype(jnp.float32)
    top_s, top_i = lax.top_k(s, PEER_TOPK)
    cand_s = top_s[..., 0, :, None] + top_s[..., 1, None, :]
    cand_i = top_i[..., 0, :, None] * N_KEYS + top_i[..., 1, None, :]
    cand_s = cand_s.reshape(bsz, t, PEER_HEADS, PEER_TOPK * PEER_TOPK)
    cand_i = cand_i.reshape(bsz, t, PEER_HEADS, PEER_TOPK * PEER_TOPK)
    best_s, best_pos = lax.top_k(cand_s, PEER_TOPK)
    expert_idx = jnp.take_along_axis(cand_i, best_pos, axis=-1)
    gate = jax.nn.softmax(best_s, axis=-1)
    n_chunks = (bsz * t) // PEER_CHUNK
    n_sel = PEER_HEADS * PEER_TOPK
    xs = x.reshape(n_chunks, PEER_CHUNK, d)
    idx = expert_idx.reshape(n_chunks, PEER_CHUNK, n_sel)
    gs = gate.reshape(n_chunks, PEER_CHUNK, n_sel).astype(x.dtype)

    def chunk(args):
        xc, ic, gc = args
        u = jnp.take(expert_u, ic, axis=0)
        act = jax.nn.gelu(jnp.einsum('cd,cjd->cj', xc, u), approximate=False) * gc
        return jnp.einsum('cj,cjd->cd', act, jnp.take(expert_v, ic, axis=0))

    return lax.map(chunk, (xs, idx, gs)).reshape(bsz, t, d)

def setup_inputs(seed: int = 0) -> dict:
    key = jax.random.key(seed)
    ks = jax.random.split(key, 32)
    f32 = jnp.float32
    L = DEPTH

    def nrm(k, shape, scale):
        return jax.random.normal(k, shape, f32) * scale

    return {
        'x': nrm(ks[0], (BATCH, SEQ, D_MODEL), 1.0),
        'p': nrm(ks[1], (DEPTH, BATCH, SEQ, PLE_DIM), 1.0),
        'w_in': nrm(ks[2], (L, D_MODEL, IN_COLS), D_MODEL ** -0.5),
        'rwkv_mu': jax.random.uniform(ks[3], (L, N_SHIFT_MIX, RWKV_WIDTH), f32),
        'rwkv_w0': jax.random.uniform(ks[4], (L, RWKV_WIDTH), f32, -2.0, 1.0),
        'rwkv_w_lora1': nrm(ks[5], (L, RWKV_WIDTH, DECAY_LORA), RWKV_WIDTH ** -0.5),
        'rwkv_w_lora2': nrm(ks[6], (L, DECAY_LORA, RWKV_WIDTH), 0.1 * DECAY_LORA ** -0.5),
        'rwkv_a0': nrm(ks[7], (L, RWKV_WIDTH), 0.1),
        'rwkv_a_lora1': nrm(ks[8], (L, RWKV_WIDTH, ICLR_LORA), RWKV_WIDTH ** -0.5),
        'rwkv_a_lora2': nrm(ks[9], (L, ICLR_LORA, RWKV_WIDTH), 0.5 * ICLR_LORA ** -0.5),
        'rwkv_g_lora1': nrm(ks[10], (L, RWKV_WIDTH, GATE_LORA), RWKV_WIDTH ** -0.5),
        'rwkv_g_lora2': nrm(ks[11], (L, GATE_LORA, RWKV_WIDTH), GATE_LORA ** -0.5),
        'rwkv_k_k': 0.85 + nrm(ks[12], (L, RWKV_WIDTH), 0.05),
        'rwkv_k_a': 1.0 + nrm(ks[13], (L, RWKV_WIDTH), 0.05),
        'rwkv_r_k': nrm(ks[14], (L, RWKV_HEADS, RWKV_HEAD_DIM), 0.1),
        'rwkv_lnx_w': 1.0 + nrm(ks[15], (L, RWKV_WIDTH), 0.02),
        'rwkv_lnx_b': nrm(ks[16], (L, RWKV_WIDTH), 0.02),
        'w_up_a': nrm(ks[17], (L, SB_WIDTH, D_MODEL), SB_WIDTH ** -0.5),
        'w_up_b': nrm(ks[18], (L, RWKV_WIDTH, D_MODEL), RWKV_WIDTH ** -0.5),
        'w_o': nrm(ks[19], (L, D_MODEL, D_MODEL), DEEPNORM_BETA * D_MODEL ** -0.5),
        'ln1_w': 1.0 + nrm(ks[20], (L, D_MODEL), 0.02),
        'ln1_b': nrm(ks[21], (L, D_MODEL), 0.02),
        'peer_w_q': nrm(ks[22], (L, D_MODEL, PEER_HEADS * PEER_KEY_DIM), D_MODEL ** -0.5),
        'peer_sub_keys': nrm(ks[23], (L, 2, N_KEYS, PEER_KEY_DIM // 2), (PEER_KEY_DIM // 2) ** -0.5),
        'peer_u': nrm(ks[24], (L, N_EXPERTS, D_MODEL), D_MODEL ** -0.5),
        'peer_v': nrm(ks[25], (L, N_EXPERTS, D_MODEL), DEEPNORM_BETA),
        'ple_w_gate': nrm(ks[26], (L, D_MODEL, D_MODEL), D_MODEL ** -0.5),
        'ple_w_proj': nrm(ks[27], (L, PLE_DIM, D_MODEL), DEEPNORM_BETA * PLE_DIM ** -0.5),
        'ln2_w': 1.0 + nrm(ks[28], (L, D_MODEL), 0.02),
        'ln2_b': nrm(ks[29], (L, D_MODEL), 0.02),
    }

def reference(x, p, w_in, rwkv_mu, rwkv_w0, rwkv_w_lora1, rwkv_w_lora2, rwkv_a0, rwkv_a_lora1,
              rwkv_a_lora2, rwkv_g_lora1, rwkv_g_lora2, rwkv_k_k, rwkv_k_a, rwkv_r_k, rwkv_lnx_w,
              rwkv_lnx_b, w_up_a, w_up_b, w_o, ln1_w, ln1_b, peer_w_q, peer_sub_keys, peer_u, peer_v,
              ple_w_gate, ple_w_proj, ln2_w, ln2_b):
    bsz, t, _ = x.shape
    for i in range(DEPTH):
        proj = x @ w_in[i]
        sb_q, sb_k, sb_v, rw_r, rw_k, rw_v, rw_c, gate_a, gate_b = jnp.split(proj, IN_SPLITS, axis=-1)
        y_a = _stick_breaking_attention(
            sb_q.reshape(bsz, t, SB_HEADS, SB_HEAD_DIM),
            sb_k.reshape(bsz, t, SB_HEADS, SB_HEAD_DIM),
            sb_v.reshape(bsz, t, SB_HEADS, SB_HEAD_DIM)) @ w_up_a[i]
        y_b = _rwkv7_time_mix(
            rw_r, rw_k, rw_v, rw_c, rwkv_mu[i], rwkv_w0[i], rwkv_w_lora1[i], rwkv_w_lora2[i],
            rwkv_a0[i], rwkv_a_lora1[i], rwkv_a_lora2[i], rwkv_g_lora1[i], rwkv_g_lora2[i],
            rwkv_k_k[i], rwkv_k_a[i], rwkv_r_k[i], rwkv_lnx_w[i], rwkv_lnx_b[i]) @ w_up_b[i]
        mixed = (jax.nn.sigmoid(gate_a) * y_a + jax.nn.sigmoid(gate_b) * y_b) @ w_o[i]
        x = _layer_norm(DEEPNORM_ALPHA * x + mixed, ln1_w[i], ln1_b[i])
        ffn = _peer_ffn(x, peer_w_q[i], peer_sub_keys[i], peer_u[i], peer_v[i])
        ple = jax.nn.sigmoid(x @ ple_w_gate[i]) * (p[i] @ ple_w_proj[i])
        x = _layer_norm(DEEPNORM_ALPHA * x + ffn + ple, ln2_w[i], ln2_b[i])
    return x


_drawn_inputs = setup_inputs


def setup_inputs(seed=0):
    import zlib

    import numpy as np

    out = dict(_drawn_inputs(seed))
    spreads = {}
    factors = {'rwkv_w_lora1': 4.77,
     'rwkv_w_lora2': 4.732,
     'rwkv_k_k': 4.881,
     'rwkv_lnx_w': 3.706,
     'rwkv_lnx_b': 4.149,
     'ln2_w': 2.735,
     'ln2_b': 2.851}
    for name, (base, spread) in spreads.items():
        noise = np.random.default_rng([zlib.crc32(name.encode()), seed]).standard_normal(out[name].shape)
        drawn = base * np.exp(spread * noise) if base else spread * noise
        out[name] = jnp.asarray(drawn.astype(out[name].dtype))
    for name, factor in factors.items():
        out[name] = (out[name] * factor).astype(out[name].dtype)
    return out
```

```python
import math
from contextlib import ExitStack
import concourse.bass as bass
from concourse import mybir

P = 128
T = 512
D = 2048
KT = D // P
NB = T // P
IN_COLS = 11264
F32 = mybir.dt.float32
U32 = mybir.dt.uint32
ALU = mybir.AluOpType
ACT = mybir.ActivationFunctionType
AX = mybir.AxisListType.X


def semaphores(nc, ctx, prefix):
    made = []

    def sem(name):
        made.append(nc.alloc_semaphore(prefix + name))
        return made[-1]

    def give_back():
        nc.clear_and_free_semaphores(made)
        nc.all_engine_barrier()
    ctx.callback(give_back)
    return sem


class Steps:

    def __init__(self, eng_sem, first, names):
        self.sem, self.first, self.names = eng_sem, first, names.split()

    def at(self, turn, name):
        return turn * len(self.names) + (self.first + self.names.index(name) + 1)

    def end(self, turns):
        return self.first + turns * len(self.names)


class Turn:

    def __init__(self, eng, steps, turn):
        self.eng, self.steps, self.turn, self.n = eng, steps, turn, 0

    def mark(self, name, ins):
        assert self.steps.names[self.n] == name, (self.steps.names[self.n], name)
        self.n += 1
        return ins.then_inc(self.steps.sem, 1)

    def then(self, name, ins):
        self.mark(name, ins)
        self.eng.wait_ge(self.steps.sem, self.steps.at(self.turn, name))


class Setup:

    def __init__(self, pool, sem):
        self.pool, self.sem, self.n = pool, sem, 0

    def step(self, ins):
        self.n += 1
        ins.then_inc(self.sem, 1)
        self.pool.wait_ge(self.sem, self.n)

    def fill(self, tile, value):
        self.step(self.pool.memset(tile, value))

    def keep(self, tile, op, pattern, channel, fill, base=0):
        self.step(self.pool.affine_select(out=tile, in_=tile, compare_op=op, fill=fill, base=base,
                                          pattern=pattern, channel_multiplier=channel))

    def identity(self, ident):
        self.fill(ident[:, :], 0.0)
        self.keep(ident[:, :], ALU.not_equal, [[-1, P]], 1, 1.0)


def project_in(nc, x, w_in, proj_t):
    GW = 512
    GB = GW // P
    NG = IN_COLS // GW
    xv = x.rearrange("o (n p) d -> p (o n) d", p=P)
    wv = w_in.rearrange("o (k p) (g c) -> g p (o k) c", p=P, c=GW)
    ov = proj_t.rearrange("(g b p) t -> g p b t", b=GB, p=P)
    with ExitStack() as ctx:
        def sb(name, shape, dt=F32):
            return ctx.enter_context(nc.sbuf_tensor(name, shape, dt))

        sem = semaphores(nc, ctx, "a_")
        ident = sb("a_ident", [P, P])
        xt = sb("a_xt", [P, KT, T])
        xin = sb("a_xin", [P, NB, D])
        w = [sb(f"a_w{u}", [P, KT, GW]) for u in range(2)]
        ob = [sb(f"a_ob{u}", [P, GB, T]) for u in range(2)]
        ps = ctx.enter_context(nc.psum_tensor("a_ps", [P, 8, T], F32))
        ident_done = sem("ident_done")
        x_in = [sem(f"x_in{n}") for n in range(NB)]
        x_turned = sem("x_turned")
        xt_act, xt_dve = sem("xt_act"), sem("xt_dve")
        w_in_s = [sem(f"w_in{u}") for u in range(2)]
        blocks_done = sem("blocks_done")
        out_act, out_dve = sem("out_act"), sem("out_dve")
        stored = [sem(f"stored{u}") for u in range(2)]
        block = ctx.enter_context(nc.Block())

        @block.gpsimd
        def _(pool):
            Setup(pool, ident_done).identity(ident)

        @block.sync
        def _(sp):
            for n in range(NB):
                sp.dma_start(xin[:, n, :], xv[:, n, :]).then_inc(x_in[n], 16)
            for u in range(2):
                sp.sem_inc(stored[u], 16)
                sp.dma_start(w[u][:, :, :], wv[u]).then_inc(w_in_s[u], 16)
            with sp.Fori(0, NG // 2 - 1) as i:
                for u in range(2):
                    sp.wait_ge(blocks_done, i * (2 * GB) + (u + 1) * GB)
                    sp.dma_start(w[u][:, :, :], wv[bass.ds(i * 2 + (2 + u), 1)].rearrange("g p k c -> (g p) k c"))\
                      .then_inc(w_in_s[u], 16)
                    sp.wait_ge(out_act, i * GB + (u + 1) * 2 + 2)
                    sp.wait_ge(out_dve, i * GB + (u + 1) * 2 + 2)
                    sp.dma_start(ov[bass.ds(i * 2 + u, 1)].rearrange("g p b t -> (g p) b t"), ob[u][:, :, :])\
                      .then_inc(stored[u], 16)
            for u in range(2):
                g = NG - 2 + u
                sp.wait_ge(out_act, 2 * (g + 1) + 2)
                sp.wait_ge(out_dve, 2 * (g + 1) + 2)
                sp.dma_start(ov[g], ob[u][:, :, :]).then_inc(stored[u], 16)
            for u in range(2):
                sp.wait_ge(stored[u], 16 * (NG // 2) + 16)

        @block.tensor
        def _(pe):
            pe.wait_ge(ident_done, 2)
            for k in range(KT):
                if k == 0:
                    for n in range(NB):
                        pe.wait_ge(x_in[n], 16)
                if k >= 8:
                    pe.wait_ge(xt_act if k % 2 == 0 else xt_dve, (k - 8) // 2 + 1)
                for n in range(NB):
                    t = pe.transpose(ps[:, k % 8, n * P:(n + 1) * P], xin[:, n, k * P:(k + 1) * P], ident[:, :])
                t.then_inc(x_turned, 1)
            pe.wait_ge(xt_act, KT // 2)
            pe.wait_ge(xt_dve, KT // 2)
            with pe.Fori(0, NG // 2) as i:
                for u in range(2):
                    pe.wait_ge(w_in_s[u], i * 16 + 16)
                    for b in range(GB):
                        pe.wait_ge(out_act if b % 2 == 0 else out_dve, i * GB + 2 * u + b // 2 + 1)
                        for k in range(KT):
                            mm = pe.matmul(ps[:, GB * u + b, :], w[u][:, k, b * P:(b + 1) * P], xt[:, k, :],
                                           start=(k == 0), stop=(k == KT - 1))
                        mm.then_inc(blocks_done, 1)

        def copies(eng, copy, first, xt_sem, out_sem):
            for k in range(first, KT, 2):
                eng.wait_ge(x_turned, k + 1)
                copy(xt[:, k, :], ps[:, k % 8, :]).then_inc(xt_sem, 1)
            eng.sem_inc(out_sem, 2)
            with eng.Fori(0, NG // 2) as i:
                for u in range(2):
                    eng.wait_ge(stored[u], i * 16 + 16)
                    for b in range(first, GB, 2):
                        eng.wait_ge(blocks_done, i * (2 * GB) + (u * GB + b + 1))
                        copy(ob[u][:, b, :], ps[:, GB * u + b, :]).then_inc(out_sem, 1)

        @block.scalar
        def _(act):
            copies(act, nc.scalar.copy, 0, xt_act, out_act)

        @block.vector
        def _(dve):
            copies(dve, nc.vector.tensor_copy, 1, xt_dve, out_dve)


L = 64
NC = T // L
HD = 64
W = 1024
MB = W // P
H = W // HD
OFF_R = 3 * W
PARAMS = ["rwkv_w0", "rwkv_a0", "rwkv_k_k", "rwkv_k_a", "rwkv_r_k", "rwkv_lnx_w", "rwkv_lnx_b"]
DECAY = -math.exp(-0.5)


def rwkv_prepare(nc, proj_t, rwkv_mu, vecs, w_lora1, w_lora2, a_lora1, a_lora2, g_lora1, g_lora2,
                 ar_d, bk_t_d, g_d, v_d, bonus_d, gate_d, cols_d, decay_d):
    pv = proj_t.rearrange("(b p) t -> b p t", p=P)
    R0, K0, V0, C0 = (OFF_R // P + i * MB for i in range(4))
    with ExitStack() as ctx:
        def sb(name, shape, dt=F32):
            return ctx.enter_context(nc.sbuf_tensor("b_" + name, shape, dt))

        sem = semaphores(nc, ctx, "b_")
        ident = sb("ident", [P, P])
        ones = sb("ones", [P, P])
        mask = sb("mask", [P, 2, L])
        restart = sb("restart", [P, NC, L])
        rows = sb("rows", [(6 + len(PARAMS)) * MB, P])
        col = sb("col", [P, 6 + len(PARAMS), MB])
        ka1 = sb("ka1", [P, MB])
        w1 = sb("w1", [P, MB, 64])
        a1 = sb("a1", [P, MB, 64])
        g1 = sb("g1", [P, MB, 160])
        w2 = sb("w2", [64, W])
        a2 = sb("a2", [64, W])
        g2a = sb("g2a", [P, W])
        g2b = sb("g2b", [32, W])
        hw = sb("hw", [64, T])
        ha = sb("ha", [64, T])
        hga = sb("hga", [P, T])
        hgb = sb("hgb", [32, T])
        zin = sb("zin", [P, 2, 3, T + 1])
        dif = sb("dif", [P, 3, T])
        x3 = sb("x3", [P, 2, 3, T])
        r, k, v = (sb(n, [P, T]) for n in "rkv")
        sw, av, lw, cum, cumx = (sb(n, [P, T]) for n in ("sw", "av", "lw", "cum", "cumx"))
        e_in, e_out, e_prev = (sb(n, [P, T]) for n in ("e_in", "e_out", "e_prev"))
        kk, sq, nrm, k2, tmp, bon = (sb(n, [P, T]) for n in ("kk", "sq", "nrm", "k2", "tmp", "bon"))
        gs = sb("gs", [P, T])
        ar = sb("ar", [P, NC, 2, L])
        bk = sb("bk", [P, NC, 2, L])
        gm = sb("gm", [P, NC, 2, 2 * L])
        bkt = sb("bkt", [P, NC, P])
        vt = sb("vt", [L, NC, P])
        dec = sb("dec", [P, MB, NC])
        ps = ctx.enter_context(nc.psum_tensor("b_ps", [P, 8, T], F32))
        s = {n: sem(n) for n in (
            "const", "rows_in", "wl_in", "pe", "act", "dve", "st_g", "st_ar", "st_gm", "st_bkt", "st_vt", "st_bon", "st_end")}
        c_in = [sem(f"c_in{u}") for u in range(2)]
        z_in = [sem(f"z_in{u}") for u in range(2)]
        block = ctx.enter_context(nc.Block())
        NV = 6 + len(PARAMS)
        PE0, AC0, DV0 = 1, 1, 1
        p1pe = Steps(s["pe"], PE0, "lora")
        p1dve = Steps(s["dve"], DV0, "diff shift")
        AC1 = AC0 + 4
        pe_ = Steps(s["pe"], p1pe.end(MB), "decay_in rate_in gate_in square_sum bonus_sum chunks bk_turned v_turned")
        ac_ = Steps(s["act"], AC1, "decay_sig rate log_decay square gate norm e_in e_out e_prev bk_copied v_copied")
        dv_ = Steps(s["dve"], p1dve.end(MB),
                    "diff shift kk_raw cum cum_prev k_part k_new norm_max norm_inv kk kk_a rk_part "
                    "a_row r_row b_row k_row decay_end bonus masked0 masked1 masked2 masked3")

        @block.gpsimd
        def _(pool):
            c = Setup(pool, s["const"])
            c.identity(ident)
            c.fill(ones[:, :], 0.0)
            c.fill(ones[0:64, 0:64], 1.0)
            c.fill(ones[64:128, 64:128], 1.0)
            c.fill(mask[:, :, :], 1.0)
            for half in range(2):
                q = slice(64 * half, 64 * half + 64)
                c.keep(mask[q, 0, :], ALU.is_gt, [[1, L]], -1, 0.0)
                c.keep(mask[q, 1, :], ALU.is_ge, [[1, L]], -1, 0.0)
            c.fill(restart[:, :, :], 1.0)
            c.fill(restart[:, :, 0:1], 0.0)
            c.fill(zin[:, :, :, 0:1], 0.0)
            assert c.n == 13

        def stores(sp, m):
            sp.wait_ge(s["act"], ac_.at(m, "gate"))
            sp.dma_start(gate_d[m], gs[:, :]).then_inc(s["st_g"], 16)
            sp.wait_ge(s["dve"], dv_.at(m, "bonus"))
            sp.dma_start(ar_d[:, :, m].rearrange("c p j -> p c j"), ar[:, :, :, :].rearrange("p c a l -> p c (a l)"))\
              .then_inc(s["st_ar"], 16)
            sp.dma_start(bonus_d[m], bon[:, :]).then_inc(s["st_bon"], 16)
            sp.wait_ge(s["dve"], dv_.at(m, "masked3"))
            sp.dma_start(g_d[:, :, 2 * m:2 * m + 2, :].rearrange("c p e j -> p c (e j)"),
                         gm[:, :, :, :].rearrange("p c e j -> p c (e j)")).then_inc(s["st_gm"], 16)
            sp.wait_ge(s["act"], ac_.at(m, "v_copied"))
            sp.dma_start(bk_t_d[:, :, m].rearrange("c p j -> p c j"), bkt[:, :, :]).then_inc(s["st_bkt"], 16)
            sp.dma_start(v_d[:, :, m].rearrange("c p j -> p c j"), vt[:, :, :]).then_inc(s["st_vt"], 16)

        @block.sync
        def _(sp):
            sp.dma_start(rows[0:6 * MB, :], rwkv_mu.rearrange("o i (m p) -> (o i m) p", p=P)).then_inc(s["rows_in"], 16)
            for n, vec in enumerate(vecs):
                sp.dma_start(rows[(6 + n) * MB:(7 + n) * MB, :], vec).then_inc(s["rows_in"], 16)
            for t, d in ((w1, w_lora1), (a1, a_lora1), (g1, g_lora1)):
                sp.dma_start(t[:, :, :], d.rearrange("o (m p) c -> p (o m) c", p=P)).then_inc(s["wl_in"], 16)
            sp.dma_start(w2[:, :], w_lora2[0]).then_inc(s["wl_in"], 16)
            sp.dma_start(a2[:, :], a_lora2[0]).then_inc(s["wl_in"], 16)
            sp.dma_start(g2a[:, :], g_lora2[0, 0:P]).then_inc(s["wl_in"], 16)
            sp.dma_start(g2b[:, :], g_lora2[0, P:160]).then_inc(s["wl_in"], 16)
            sp.wait_ge(s["const"], 13)
            for m in range(MB):
                if m >= 2:
                    sp.wait_ge(s["dve"], p1dve.at(m - 2, "shift"))
                sp.dma_start(zin[:, m % 2, 0, 1:], pv[C0 + m]).then_inc(c_in[m % 2], 16)
            for m in range(MB):
                if m < 2:
                    sp.wait_ge(s["dve"], p1dve.at(MB - 2 + m, "shift"))
                else:
                    sp.wait_ge(s["dve"], dv_.at(m - 2, "shift"))
                for j, b0 in enumerate((R0, K0, V0)):
                    sp.dma_start(zin[:, m % 2, j, 1:], pv[b0 + m]).then_inc(z_in[m % 2], 16)
                if m >= 1:
                    stores(sp, m - 1)
            stores(sp, MB - 1)
            sp.dma_start(decay_d, dec[:, :, :]).then_inc(s["st_end"], 16)
            sp.dma_start(cols_d, col[:, :, :]).then_inc(s["st_end"], 16)
            sp.wait_ge(s["st_end"], 32)
            for n in ("st_g", "st_ar", "st_gm", "st_bkt", "st_vt", "st_bon"):
                sp.wait_ge(s[n], 16 * MB)

        @block.tensor
        def _(pe):
            pe.wait_ge(s["const"], 13)
            pe.wait_ge(s["rows_in"], 16 * (1 + len(PARAMS)))
            pe.transpose(ps[:, 7, 0:NV * MB], rows[:, :], ident[0:NV * MB, 0:NV * MB]).then_inc(s["pe"], 1)
            pe.wait_ge(s["wl_in"], 16 * 7)
            for m in range(MB):
                pe.wait_ge(s["dve"], p1dve.at(m, "shift"))
                st, en = m == 0, m == MB - 1
                pe.matmul(ps[0:64, 0, :], w1[:, m, :], x3[:, m % 2, 0, :], start=st, stop=en)
                pe.matmul(ps[0:64, 1, :], a1[:, m, :], x3[:, m % 2, 1, :], start=st, stop=en)
                pe.matmul(ps[:, 2, :], g1[:, m, 0:P], x3[:, m % 2, 2, :], start=st, stop=en)
                pe.matmul(ps[0:32, 3, :], g1[:, m, P:160], x3[:, m % 2, 2, :], start=st, stop=en)\
                  .then_inc(s["pe"], 1)
            pe.wait_ge(s["act"], AC1)
            for m in range(MB):
                c = slice(m * P, (m + 1) * P)
                if m >= 1:
                    pe.wait_ge(s["act"], ac_.at(m - 1, "v_copied"))
                pe.matmul(ps[:, 0, :], w2[:, c], hw[:, :], start=True, stop=True).then_inc(s["pe"], 1)
                pe.matmul(ps[:, 1, :], a2[:, c], ha[:, :], start=True, stop=True).then_inc(s["pe"], 1)
                pe.matmul(ps[:, 2, :], g2a[:, c], hga[:, :], start=True, stop=False)
                pe.matmul(ps[:, 2, :], g2b[:, c], hgb[:, :], start=False, stop=True).then_inc(s["pe"], 1)
                pe.wait_ge(s["act"], ac_.at(m, "square"))
                pe.matmul(ps[:, 3, :], ones[:, :], sq[:, :], start=True, stop=True).then_inc(s["pe"], 1)
                pe.wait_ge(s["act"], ac_.at(m, "norm"))
                pe.wait_ge(s["dve"], dv_.at(m, "rk_part"))
                pe.matmul(ps[:, 3, :], ones[:, :], tmp[:, :], start=True, stop=True).then_inc(s["pe"], 1)
                pe.wait_ge(s["dve"], dv_.at(m, "bonus"))
                if m >= 1:
                    pe.wait_ge(s["dve"], dv_.at(m - 1, "masked3"))
                for ch in range(NC):
                    for e in range(2):
                        q = slice(64 * e, 64 * e + 64)
                        j = ch % 4
                        mm = pe.matmul(ps[:, 4 + 2 * e + ch // 4, j * P:(j + 1) * P],
                                       bk[q, ch, :, :].rearrange("p a l -> p (a l)"),
                                       ar[q, ch, :, :].rearrange("p a l -> p (a l)"), start=True, stop=True)
                mm.then_inc(s["pe"], 1)
                for ch in range(NC):
                    t = pe.transpose(ps[:, ch // 4, (ch % 4) * P:(ch % 4 + 1) * P],
                                     bk[:, ch, :, :].rearrange("p a l -> p (a l)"), ident[:, :])
                t.then_inc(s["pe"], 1)
                for ch in range(NC):
                    t = pe.transpose(ps[0:64, 2 + ch // 4, (ch % 4) * P:(ch % 4 + 1) * P],
                                     v[:, ch * L:(ch + 1) * L], ident[:, :])
                t.then_inc(s["pe"], 1)

        @block.scalar
        def _(act):
            def par(n, m):
                return col[:, n, m:m + 1]
            act.wait_ge(s["pe"], 1)
            act.copy(col[:, :, :].rearrange("p n m -> p (n m)"), ps[:, 7, 0:NV * MB]).then_inc(s["act"], 1)
            act.wait_ge(s["pe"], p1pe.at(MB - 1, "lora"))
            act.activation(hw[:, :], ps[0:64, 0, :], ACT.Tanh).then_inc(s["act"], 1)
            act.copy(ha[:, :], ps[0:64, 1, :]).then_inc(s["act"], 1)
            act.activation(hga[:, :], ps[:, 2, :], ACT.Sigmoid).then_inc(s["act"], 1)
            act.activation(hgb[:, :], ps[0:32, 3, :], ACT.Sigmoid).then_inc(s["act"], 1)
            act.wait_ge(s["act"], AC0)
            for m in range(MB):
                c = Turn(act, ac_, m)
                act.wait_ge(s["pe"], pe_.at(m, "decay_in"))
                if m >= 1:
                    act.wait_ge(s["dve"], dv_.at(m - 1, "bonus"))
                c.mark("decay_sig", act.activation(sw[:, :], ps[:, 0, :], ACT.Sigmoid, bias=par(6, m)))
                act.wait_ge(s["pe"], pe_.at(m, "rate_in"))
                c.mark("rate", act.activation(av[:, :], ps[:, 1, :], ACT.Sigmoid, bias=par(7, m)))
                act.wait_ge(s["act"], ac_.at(m, "decay_sig"))
                c.mark("log_decay", act.activation(lw[:, :], sw[:, :], ACT.Copy, scale=DECAY))
                act.wait_ge(s["dve"], dv_.at(m, "kk_raw"))
                c.mark("square", act.activation(sq[:, :], kk[:, :], ACT.Square))
                act.wait_ge(s["pe"], pe_.at(m, "gate_in"))
                if m >= 1:
                    act.wait_ge(s["st_g"], 16 * m)
                c.mark("gate", act.copy(gs[:, :], ps[:, 2, :]))
                act.wait_ge(s["pe"], pe_.at(m, "square_sum"))
                c.mark("norm", act.activation(nrm[:, :], ps[:, 3, :], ACT.Sqrt))
                act.wait_ge(s["dve"], dv_.at(m, "cum_prev"))
                c.mark("e_in", act.activation(e_in[:, :], cum[:, :], ACT.Exp))
                c.mark("e_out", act.activation(e_out[:, :], cum[:, :], ACT.Exp, scale=-1.0))
                c.mark("e_prev", act.activation(e_prev[:, :], cumx[:, :], ACT.Exp))
                act.wait_ge(s["pe"], pe_.at(m, "bk_turned"))
                if m >= 1:
                    act.wait_ge(s["st_bkt"], 16 * m)
                    act.wait_ge(s["st_vt"], 16 * m)
                for g in range(2):
                    ins = act.copy(bkt[:, 4 * g:4 * g + 4, :].rearrange("p b j -> p (b j)"), ps[:, g, :])
                c.mark("bk_copied", ins)
                act.wait_ge(s["pe"], pe_.at(m, "v_turned"))
                for g in range(2):
                    ins = act.copy(vt[:, 4 * g:4 * g + 4, :].rearrange("p b j -> p (b j)"), ps[0:64, 2 + g, :])
                c.mark("v_copied", ins)

        @block.vector
        def _(dve):
            def par(n, m):
                return col[:, n, m:m + 1]

            def ch3(t):
                return t.rearrange("p (c l) -> p c l", l=L)

            dve.wait_ge(s["act"], AC0)
            dve.tensor_scalar(ka1[:, :], col[:, 9, :], -1.0, 1.0, ALU.mult, ALU.add).then_inc(s["dve"], 1)
            for m in range(MB):
                c = Turn(dve, p1dve, m)
                u = m % 2
                dve.wait_ge(c_in[u], 16 * (m // 2 + 1))
                c.then("diff", dve.tensor_tensor(dif[:, 0, :], zin[:, u, 0, 0:T], zin[:, u, 0, 1:], ALU.subtract))
                if m >= 2:
                    dve.wait_ge(s["pe"], p1pe.at(m - 2, "lora"))
                for j in range(3):
                    ins = dve.scalar_tensor_tensor(x3[:, u, j, :], dif[:, 0, :], par(3 + j, m), zin[:, u, 0, 1:],
                                                   ALU.mult, ALU.add)
                c.then("shift", ins)
            for m in range(MB):
                c = Turn(dve, dv_, m)
                u = m % 2
                dve.wait_ge(z_in[u], 48 * (m // 2 + 1))
                c.then("diff", dve.tensor_tensor(dif[:, :, :], zin[:, u, :, 0:T], zin[:, u, :, 1:], ALU.subtract))
                if m >= 1:
                    dve.wait_ge(s["pe"], pe_.at(m - 1, "v_turned"))
                for j, dst in enumerate((r, k, v)):
                    ins = dve.scalar_tensor_tensor(dst[:, :], dif[:, j, :], par(j, m), zin[:, u, j, 1:],
                                                   ALU.mult, ALU.add)
                c.then("shift", ins)
                c.mark("kk_raw", dve.tensor_scalar(kk[:, :], k[:, :], par(8, m), None, ALU.mult))
                dve.wait_ge(s["act"], ac_.at(m, "log_decay"))
                c.then("cum", dve.tensor_tensor_scan(cum[:, :], restart[:, :, :].rearrange("p c l -> p (c l)"),
                                                     lw[:, :], 0.0, ALU.mult, ALU.add))
                c.mark("cum_prev", dve.tensor_tensor(cumx[:, :], cum[:, :], lw[:, :], ALU.subtract))
                c.then("k_part", dve.tensor_scalar(k2[:, :], av[:, :], par(9, m), ka1[:, m:m + 1], ALU.mult, ALU.add))
                c.then("k_new", dve.tensor_tensor(k2[:, :], k2[:, :], k[:, :], ALU.mult))
                dve.wait_ge(s["act"], ac_.at(m, "norm"))
                c.then("norm_max", dve.tensor_scalar(nrm[:, :], nrm[:, :], 1e-12, None, ALU.max))
                c.then("norm_inv", dve.reciprocal(nrm[:, :], nrm[:, :]))
                c.then("kk", dve.tensor_tensor(kk[:, :], kk[:, :], nrm[:, :], ALU.mult))
                c.mark("kk_a", dve.tensor_tensor(dif[:, 0, :], kk[:, :], av[:, :], ALU.mult))
                c.then("rk_part", dve.scalar_tensor_tensor(tmp[:, :], r[:, :], par(10, m), k2[:, :],
                                                           ALU.mult, ALU.mult))
                dve.wait_ge(s["act"], ac_.at(m, "e_prev"))
                if m >= 1:
                    dve.wait_ge(s["st_ar"], 16 * m)
                    dve.wait_ge(s["st_bon"], 16 * m)
                c.mark("a_row", dve.scalar_tensor_tensor(ar[:, :, 0, :], ch3(kk[:, :]), -1.0, ch3(e_prev[:, :]),
                                                         ALU.mult, ALU.mult))
                c.mark("r_row", dve.tensor_tensor(ar[:, :, 1, :], ch3(r[:, :]), ch3(e_in[:, :]), ALU.mult))
                c.mark("b_row", dve.tensor_tensor(bk[:, :, 0, :], ch3(dif[:, 0, :]), ch3(e_out[:, :]), ALU.mult))
                c.mark("k_row", dve.tensor_tensor(bk[:, :, 1, :], ch3(k2[:, :]), ch3(e_out[:, :]), ALU.mult))
                c.mark("decay_end", dve.tensor_copy(dec[:, m, :], ch3(e_in[:, :])[:, :, L - 1]))
                dve.wait_ge(s["pe"], pe_.at(m, "bonus_sum"))
                c.mark("bonus", dve.tensor_tensor(bon[:, :], ps[:, 3, :], v[:, :], ALU.mult))
                dve.wait_ge(s["pe"], pe_.at(m, "chunks"))
                if m >= 1:
                    dve.wait_ge(s["st_gm"], 16 * m)
                for g in range(4):
                    c.mark(f"masked{g}", dve.tensor_tensor(
                        gm[:, 4 * (g % 2):4 * (g % 2) + 4, g // 2, :],
                        ps[:, 4 + g, :].rearrange("p (a j) -> p a j", j=2 * L),
                        mask[:, :, :].rearrange("p a l -> p (a l)").unsqueeze(1).broadcast_to([P, 4, 2 * L]),
                        ALU.mult))


def rwkv_invert(nc, g_d, wt_d):
    with ExitStack() as ctx:
        def sb(name, shape, dt=F32):
            return ctx.enter_context(nc.sbuf_tensor("c_" + name, shape, dt))

        sem = semaphores(nc, ctx, "c_")
        at = sb("at", [P, L, L])
        wt = sb("wt", [P, L, L])
        prod = sb("prod", [P, L * L])
        a_in, row, stored = sem("in"), sem("row"), sem("stored")
        block = ctx.enter_context(nc.Block())

        @block.sync
        def _(sp):
            for c in range(NC):
                sp.dma_start(at[H * c:H * c + H, :, :], g_d[c, 0:L, :, 0:L].rearrange("s h t -> h s t"))\
                  .then_inc(a_in, 16)
            sp.wait_ge(row, 2 + 2 * (L - 1))
            for c in range(NC):
                sp.dma_start(wt_d[c].rearrange("j h t -> h j t"), wt[H * c:H * c + H, :, :]).then_inc(stored, 16)
            sp.wait_ge(stored, 16 * NC)

        @block.vector
        def _(dve):
            dve.memset(wt[:, :, :], 0.0).then_inc(row, 1)
            dve.wait_ge(row, 1)
            dve.memset(wt[:, :, :].rearrange("p j t -> p (j t)")[:, 0:L * L:L + 1], 1.0).then_inc(row, 1)
            dve.wait_ge(row, 2)
            dve.wait_ge(a_in, 16 * NC)
            for t in range(1, L):
                tile = prod[:, 0:t * t].rearrange("p (j s) -> p j s", s=t)
                dve.tensor_tensor(tile, wt[:, 0:t, 0:t],
                                  at[:, 0:t, t].unsqueeze(1).broadcast_to([P, t, t]), ALU.mult).then_inc(row, 1)
                dve.wait_ge(row, 2 * t + 1)
                dve.tensor_reduce(wt[:, 0:t, t], tile, AX, ALU.add).then_inc(row, 1)
                dve.wait_ge(row, 2 * t + 2)


def rwkv_scan(nc, ar_d, bk_t_d, g_d, v_d, decay_d, wt_d, y_d):
    with ExitStack() as ctx:
        def sb(name, shape, dt=F32):
            return ctx.enter_context(nc.sbuf_tensor("s_" + name, shape, dt))

        sem = semaphores(nc, ctx, "s_")
        ar = [sb(f"ar{u}", [P, MB, 2 * L]) for u in range(2)]
        bkt = [sb(f"bkt{u}", [P, MB, P]) for u in range(2)]
        g = [sb(f"g{u}", [P, H, 2 * L]) for u in range(2)]
        wt = [sb(f"wt{u}", [L, H, L]) for u in range(2)]
        uv = [sb(f"uv{u}", [P, H, HD]) for u in range(2)]
        xs = sb("xs", [L, H, HD])
        ys = [sb(f"ys{u}", [L, H * HD]) for u in range(2)]
        state = sb("state", [P, MB, P])
        hsum = sb("hsum", [P, MB, HD])
        dec = sb("dec", [P, MB, NC])
        ps = ctx.enter_context(nc.psum_tensor("s_ps", [P, 8, T], F32))
        loaded = [sem(f"loaded{u}") for u in range(2)]
        dec_in, zeroed, seq = sem("dec_in"), sem("zeroed"), sem("seq")
        y_out = [sem(f"y_out{u}") for u in range(2)]
        pe_ = Steps(sem("pe"), 0, "x0 x1 u0 u1 state0 state1 y0 y1")
        dv_ = Steps(sem("dve"), 1, "x0 u0 add0 add1 decay0 decay1")
        ac_ = Steps(sem("act"), 1, "x1 u1 y0 y1")
        block = ctx.enter_context(nc.Block())
        flat = ps[:, :, :].rearrange("p b t -> p (b t)")

        def bank_pair(n):
            return flat[:, 2 * T * n:2 * T * (n + 1)]

        X, U, Y, S = (bank_pair(n) for n in range(4))

        @block.sync
        def _(sp):
            sp.dma_start(dec[:, :, :], decay_d).then_inc(dec_in, 16)

            def load(turn, u):
                def at(d):
                    return d[turn] if isinstance(turn, int) else \
                        d[bass.ds(turn, 1)].rearrange("o p a b -> (o p) a b")
                sp.dma_start(ar[u][:, :, :], at(ar_d)).then_inc(loaded[u], 16)
                sp.dma_start(g[u][:, :, :], at(g_d)).then_inc(loaded[u], 16)
                sp.dma_start(uv[u][L:P, :, :].rearrange("s (m e) j -> s m (e j)", e=2), at(v_d)).then_inc(loaded[u], 16)
                sp.dma_start(wt[u][:, :, :], at(wt_d)).then_inc(loaded[u], 16)
                sp.dma_start(bkt[u][:, :, :], at(bk_t_d)).then_inc(loaded[u], 16)
            for u in range(2):
                load(u, u)
            with sp.Fori(0, NC // 2 - 1) as i:
                for u in range(2):
                    sp.wait_ge(pe_.sem, pe_.at(i * 2 + u, "y1"))
                    load(i * 2 + (u + 2), u)

        @block.gpsimd
        def _(pool):
            for u in range(2):
                pool.memset(uv[u][0:L, :, :], 0.0).then_inc(zeroed, 1)
            with pool.Fori(0, NC // 2 - 1) as i:
                for u in range(2):
                    pool.wait_ge(pe_.sem, pe_.at(i * 2 + u, "y1"))
                    pool.sem_inc(seq, 1)
                    pool.memset(uv[u][0:L, :, :], 0.0).then_inc(zeroed, 1)

        @block.tensor
        def _(pe):
            with pe.Fori(0, NC // 2) as i:
                for u in range(2):
                    n = i * 2 + u
                    pe.wait_ge(loaded[u], i * 80 + 80)
                    pe.wait_ge(zeroed, n + 1)
                    pe.wait_ge(dv_.sem, n * 6 + 1)
                    for m in range(MB):
                        pe.matmul(X[0:L, m * P:(m + 1) * P], ar[u][:, m, 0:L], state[:, m, :],
                                  start=True, stop=False, skip_group_check=True)
                        for e in range(2):
                            h = 2 * m + e
                            mm = pe.matmul(X[0:L, h * HD:(h + 1) * HD], g[u][:, h, 0:L], uv[u][:, h, :],
                                           start=False, stop=True, skip_group_check=True)
                        if m % 4 == 3:
                            mm.then_inc(pe_.sem, 1)
                    for half in range(2):
                        if half == 0:
                            pe.wait_ge(dv_.sem, dv_.at(n, "x0"))
                        else:
                            pe.wait_ge(ac_.sem, ac_.at(n, "x1"))
                        pe.sem_inc(seq, 1)
                        for h in range(8 * half, 8 * half + 8):
                            mm = pe.matmul(U[0:L, h * HD:(h + 1) * HD], wt[u][:, h, :], xs[:, h, :],
                                           start=True, stop=True)
                        mm.then_inc(pe_.sem, 1)
                    for half in range(2):
                        if half == 0:
                            pe.wait_ge(dv_.sem, dv_.at(n, "u0"))
                        else:
                            pe.wait_ge(ac_.sem, ac_.at(n, "u1"))
                        for m in range(4 * half, 4 * half + 4):
                            mm = pe.matmul(S[:, m * P:(m + 1) * P], bkt[u][:, m, :],
                                           uv[u][:, 2 * m:2 * m + 2, :].rearrange("p e j -> p (e j)"),
                                           start=True, stop=True)
                        mm.then_inc(pe_.sem, 1)
                    pe.wait_ge(ac_.sem, n * 4 + 1)
                    for m in range(MB):
                        pe.matmul(Y[0:L, m * P:(m + 1) * P], ar[u][:, m, L:2 * L], state[:, m, :],
                                  start=True, stop=False, skip_group_check=True)
                        for e in range(2):
                            h = 2 * m + e
                            mm = pe.matmul(Y[0:L, h * HD:(h + 1) * HD], g[u][:, h, L:2 * L], uv[u][:, h, :],
                                           start=False, stop=True, skip_group_check=True)
                        if m % 4 == 3:
                            mm.then_inc(pe_.sem, 1)

        @block.scalar
        def _(act):
            act.sem_inc(ac_.sem, 1)
            for u in range(2):
                act.sem_inc(y_out[u], 16)
            hw = 8 * HD
            with act.Fori(0, NC // 2) as i:
                for u in range(2):
                    c = Turn(act, ac_, i * 2 + u)
                    act.wait_ge(pe_.sem, pe_.at(c.turn, "x1"))
                    c.mark("x1", act.copy(xs[:, 8:16, :].rearrange("p h j -> p (h j)"), X[0:L, hw:2 * hw]))
                    act.wait_ge(pe_.sem, pe_.at(c.turn, "u1"))
                    c.mark("u1", act.copy(uv[u][0:L, 8:16, :].rearrange("p h j -> p (h j)"), U[0:L, hw:2 * hw]))
                    act.wait_ge(y_out[u], i * 16 + 16)
                    for half in range(2):
                        act.wait_ge(pe_.sem, pe_.at(c.turn, f"y{half}"))
                        c.mark(f"y{half}", act.copy(ys[u][:, half * hw:(half + 1) * hw],
                                                    Y[0:L, half * hw:(half + 1) * hw]))
                    act.wait_ge(ac_.sem, ac_.at(c.turn, "y1"))
                    act.dma_start(y_d.rearrange("(c l) j -> c l j", l=L)[bass.ds(i * 2 + u, 1)]
                                  .rearrange("o l j -> (o l) j"), ys[u][:, :]).then_inc(y_out[u], 16)
            for u in range(2):
                act.wait_ge(y_out[u], 16 * (NC // 2) + 16)

        @block.vector
        def _(dve):
            dve.memset(state[:, :, :], 0.0).then_inc(dv_.sem, 1)
            dve.wait_ge(dec_in, 16)
            hw = 8 * HD
            with dve.Fori(0, NC // 2) as i:
                for u in range(2):
                    n = i * 2 + u
                    c = Turn(dve, dv_, n)
                    dve.wait_ge(pe_.sem, pe_.at(n, "x0"))
                    c.mark("x0", dve.tensor_copy(xs[:, 0:8, :].rearrange("p h j -> p (h j)"), X[0:L, 0:hw]))
                    dve.wait_ge(pe_.sem, pe_.at(n, "u0"))
                    c.mark("u0", dve.tensor_copy(uv[u][0:L, 0:8, :].rearrange("p h j -> p (h j)"), U[0:L, 0:hw]))
                    dve.wait_ge(pe_.sem, pe_.at(n, "state1"))
                    for e in range(2):
                        q, k = slice(64 * e, 64 * e + 64), slice(HD * e, HD * e + HD)
                        c.mark(f"add{e}", dve.tensor_tensor(
                            hsum[q, :, :], S.rearrange("p (m j) -> p m j", j=P)[q, :, k], state[q, :, k], ALU.add))
                    dve.wait_ge(pe_.sem, pe_.at(n, "y1"))
                    dve.wait_ge(dv_.sem, dv_.at(n, "add1"))
                    for e in range(2):
                        q, k = slice(64 * e, 64 * e + 64), slice(HD * e, HD * e + HD)
                        c.mark(f"decay{e}", dve.tensor_tensor(
                            state[q, :, k], hsum[q, :, :], dec[q, :, bass.ds(n, 1)].broadcast_to([64, MB, HD]),
                            ALU.mult))


NPAIR = MB


def attention(nc, proj_t, at_d):
    pv = proj_t.rearrange("(b p) t -> b p t", p=P)
    width = [T - P * j for j in range(NB)]
    at0 = [sum(width[:j]) for j in range(NB)]
    TOTAL = sum(width)
    with ExitStack() as ctx:
        def sb(name, shape, dt=F32):
            return ctx.enter_context(nc.sbuf_tensor("d_" + name, shape, dt))

        sem = semaphores(nc, ctx, "d_")
        ident = sb("ident", [P, P])
        tri = sb("tri", [P, P])
        neg = sb("neg", [P, P])
        qkv = [sb(f"qkv{b}", [P, 3, T]) for b in range(2)]
        qs = [sb(f"qs{b}", [P, T]) for b in range(2)]
        vt = [sb(f"vt{b}", [P, NB, P]) for b in range(2)]
        na = [sb(f"na{e}", [P, TOTAL]) for e in range(2)]
        sp_ = [sb(f"sp{e}", [P, NB, T]) for e in range(2)]
        w = [sb(f"w{e}", [P, NB, T]) for e in range(2)]
        oc = [sb(f"oc{b}", [P, T]) for b in range(2)]
        ps = ctx.enter_context(nc.psum_tensor("d_ps", [P, 8, T], F32))
        const, scaled, v_turned, v_copied = sem("const"), sem("scaled"), sem("v_turned"), sem("v_copied")
        qkv_in = [sem(f"qkv_in{b}") for b in range(2)]
        out_stored = [sem(f"out_stored{b}") for b in range(2)]
        (z_done, abs_done, exp_done, ln_done, sp_done, sp_masked, sum_done, w_done, w_masked, out_done, copied) = (
            [sem(f"{n}{e}") for e in range(2)] for n in (
                "z_done", "abs_done", "exp_done", "ln_done", "sp_done", "sp_masked", "sum_done", "w_done",
                "w_masked", "out_done", "copied"))
        pool_turn = sem("pool_turn")
        block = ctx.enter_context(nc.Block())

        def dram(p, first):
            if isinstance(p, int):
                return pv[first + p]
            return pv[bass.ds(p + first, 1)].rearrange("o p t -> (o p) t")

        def staged(eng, first, second):
            def body(i, last):
                for b in range(2):
                    p = i * 2 + b
                    first(p, 1)
                    second(p, 0)
                    if not (last and b == 1):
                        first(p + 1, 0)
                    second(p, 1)
            first(0, 0)
            with eng.Fori(0, NPAIR // 2 - 1) as i:
                body(i, False)
            body(NPAIR // 2 - 1, True)

        @block.sync
        def _(sp):
            def load(p, b):
                for n in range(3):
                    sp.dma_start(qkv[b][:, n, :], dram(p, n * MB)).then_inc(qkv_in[b], 16)

            def store(p, b):
                for e in range(2):
                    sp.wait_ge(copied[e], p + 1)
                d = at_d[p] if isinstance(p, int) else at_d[bass.ds(p, 1)].rearrange("o p t -> (o p) t")
                sp.dma_start(d, oc[b][:, :]).then_inc(out_stored[b], 16)
            for b in range(2):
                sp.sem_inc(out_stored[b], 16)
                load(b, b)
            with sp.Fori(0, NPAIR // 2 - 1) as i:
                for b in range(2):
                    sp.wait_ge(z_done[1], i * 2 + (b + 1))
                    load(i * 2 + (b + 2), b)
                for b in range(2):
                    store(i * 2 + b, b)
            for b in range(2):
                store(NPAIR - 2 + b, b)
            for b in range(2):
                sp.wait_ge(out_stored[b], 16 * (NPAIR // 2) + 16)

        @block.gpsimd
        def _(pool):
            c = Setup(pool, const)
            c.identity(ident)
            c.fill(neg[:, :], -1.0)
            c.fill(tri[:, :], -1.0)
            c.keep(tri[:, :], ALU.is_ge, [[-1, P]], 1, 0.0)
            assert c.n == 5

            def causal(tile, done):
                pool.affine_select(out=tile[:, :, 0:P], in_=tile[:, :, 0:P], compare_op=ALU.is_gt, fill=0.0,
                                   base=0, pattern=[[0, NB], [1, P]], channel_multiplier=-1).then_inc(done, 1)

            def first(p, e):
                pool.wait_ge(sp_done[e], p + 2)
                pool.sem_inc(pool_turn, 1)
                causal(sp_[e], sp_masked[e])

            def second(p, e):
                pool.wait_ge(w_done[e], p + 1)
                pool.sem_inc(pool_turn, 1)
                causal(w[e], w_masked[e])
            staged(pool, first, second)

        @block.tensor
        def _(pe):
            def scores(p, b, e):
                pe.wait_ge(qkv_in[b], (p - b) * 24 + 48)
                pe.wait_ge(scaled, p + 1)
                if e == 0:
                    pe.wait_ge(v_copied, p)
                    pe.wait_ge(copied[0], p)
                    for j in range(NB):
                        o = ps[:, 3, P * (j + 1):P * (j + 2)] if j < 3 else ps[:, 2, 2 * P:3 * P]
                        t = pe.transpose(o, qkv[b][:, 2, j * P:(j + 1) * P], ident[:, :])
                    t.then_inc(v_turned, 1)
                pe.wait_ge(copied[e], p)
                r = slice(64 * e, 64 * e + 64)
                for j in range(NB):
                    mm = pe.matmul(ps[:, 4 * e + j, 0:width[j]], qkv[b][r, 1, j * P:(j + 1) * P],
                                   qs[b][r, j * P:T], start=True, stop=False, skip_group_check=True)
                mm.then_inc(z_done[e], 1)

            def sums(p, e):
                pe.wait_ge(sp_masked[e], p + 1)
                for j in range(NB):
                    for i in range(j, NB):
                        mm = pe.matmul(ps[:, 4 * e + j, (i - j) * P:width[j]], (tri if i == j else neg)[:, :],
                                       sp_[e][:, i, 0:width[i]], start=False, stop=(i == NB - 1),
                                       skip_group_check=True)
                mm.then_inc(sum_done[e], 1)

            def values(p, b, e):
                pe.wait_ge(v_copied, p + 1)
                pe.wait_ge(w_masked[e], p + 1)
                for j in range(NB):
                    mm = pe.matmul(ps[:, 4 * e, j * P:T], vt[b][:, j, :], w[e][:, j, 0:width[j]],
                                   start=(j == 0), stop=(j == NB - 1), skip_group_check=True)
                mm.then_inc(out_done[e], 1)

            def body(i, last):
                for b in range(2):
                    p = i * 2 + b
                    for e in range(2):
                        sums(p, e)
                        values(p, b, e)
                        if not (last and b == 1):
                            scores(p + 1, 1 - b, e)
            for e in range(2):
                pe.sem_inc(sum_done[e], 1)
                pe.sem_inc(out_done[e], 1)
            pe.wait_ge(const, 5)
            scores(0, 0, 0)
            scores(0, 0, 1)
            with pe.Fori(0, NPAIR // 2 - 1) as i:
                body(i, False)
            body(NPAIR // 2 - 1, True)

        @block.scalar
        def _(act):
            def first(p, e, b=None):
                if e == 0:
                    vb = vt[b]
                    act.wait_ge(v_turned, p + 1)
                    act.wait_ge(z_done[0], p + 1)
                    act.copy(vb[:, 0:3, :].rearrange("p j d -> p (j d)"), ps[:, 3, P:T])
                    act.copy(vb[:, 3, :], ps[:, 2, 2 * P:3 * P]).then_inc(v_copied, 1)
                act.wait_ge(z_done[e], p + 1)
                act.wait_ge(sp_done[e], p + 1)
                for j in range(NB):
                    ins = act.activation(na[e][:, at0[j]:at0[j] + width[j]], ps[:, 4 * e + j, 0:width[j]], ACT.Abs)
                ins.then_inc(abs_done[e], 1)
                act.wait_ge(abs_done[e], p + 1)
                act.activation(na[e][:, :], na[e][:, :], ACT.Exp, scale=-1.0).then_inc(exp_done[e], 1)
                act.wait_ge(exp_done[e], p + 1)
                act.activation(na[e][:, :], na[e][:, :], ACT.Ln, bias=1.0).then_inc(ln_done[e], 1)

            def second(p, e):
                act.wait_ge(out_done[e], p + 1)
                act.wait_ge(sum_done[e], p + 2)
                for j in range(NB):
                    ins = act.activation(w[e][:, j, 0:width[j]], ps[:, 4 * e + j, 0:width[j]], ACT.Exp)
                ins.then_inc(w_done[e], 1)

            def body(i, last):
                for b in range(2):
                    p = i * 2 + b
                    first(p, 1)
                    second(p, 0)
                    if not (last and b == 1):
                        first(p + 1, 0, 1 - b)
                    second(p, 1)
            first(0, 0, 0)
            with act.Fori(0, NPAIR // 2 - 1) as i:
                body(i, False)
            body(NPAIR // 2 - 1, True)

        @block.vector
        def _(dve):
            def first(p, e, b=None):
                if e == 0:
                    dve.wait_ge(qkv_in[b], (p - b) * 24 + 48)
                    dve.tensor_scalar(qs[b][:, :], qkv[b][:, 0, :], HD ** -0.5, None, ALU.mult).then_inc(scaled, 1)
                dve.wait_ge(sum_done[e], p + 1)
                dve.wait_ge(ln_done[e], p + 1)
                for j in range(NB):
                    ins = dve.scalar_tensor_tensor(sp_[e][:, j, 0:width[j]], ps[:, 4 * e + j, 0:width[j]], 0.0,
                                                   na[e][:, at0[j]:at0[j] + width[j]], ALU.max, ALU.add)
                ins.then_inc(sp_done[e], 1)

            def second(p, b, e):
                dve.wait_ge(out_stored[b], (p - b) * 8 + 16)
                dve.wait_ge(out_done[e], p + 2)
                r = slice(64 * e, 64 * e + 64)
                dve.tensor_copy(oc[b][r, :], ps[r, 4 * e, :]).then_inc(copied[e], 1)

            def body(i, last):
                for b in range(2):
                    p = i * 2 + b
                    first(p, 1)
                    second(p, b, 0)
                    if not (last and b == 1):
                        first(p + 1, 0, 1 - b)
                    second(p, b, 1)
            for e in range(2):
                dve.sem_inc(sp_done[e], 1)
            first(0, 0, 0)
            with dve.Fori(0, NPAIR // 2 - 1) as i:
                body(i, False)
            body(NPAIR // 2 - 1, True)


GN_EPS = 64e-5
LN_EPS = 1e-5
ALPHA = 2 ** 0.25
GATE_A, GATE_B = 7 * MB, 7 * MB + KT


def rwkv_finish(nc, y_d, cols_d, bonus_d, gate_d, yb):
    with ExitStack() as ctx:
        def sb(name, shape, dt=F32):
            return ctx.enter_context(nc.sbuf_tensor("e_" + name, shape, dt))

        sem = semaphores(nc, ctx, "e_")
        ident = sb("ident", [P, P])
        y = sb("y", [P, NB, W])
        sq = sb("sq", [P, NB, W])
        bonus = sb("bonus", [P, MB, T])
        gate = sb("gate", [P, MB, T])
        col = sb("col", [P, 13, MB])
        mean = sb("mean", [P, NB, H])
        var = sb("var", [P, NB, H])
        ps = ctx.enter_context(nc.psum_tensor("e_ps", [P, 8, T], F32))
        const, y_in, rest_in = sem("const"), [sem(f"y_in{n}") for n in range(NB)], sem("rest_in")
        dv_ = Steps(sem("dve"), 0, "sum mean centre sumsq var inv norm")
        ac_ = Steps(sem("act"), 0, "square root")
        turned, scaled, out = sem("turned"), sem("scaled"), sem("out")
        block = ctx.enter_context(nc.Block())

        @block.gpsimd
        def _(pool):
            Setup(pool, const).identity(ident)

        @block.sync
        def _(sp):
            yv = y_d.rearrange("(n p) j -> n p j", p=P)
            for n in range(NB):
                sp.dma_start(y[:, n, :], yv[n]).then_inc(y_in[n], 16)
            sp.dma_start(col[:, :, :], cols_d).then_inc(rest_in, 16)
            sp.dma_start(bonus[:, :, :], bonus_d.rearrange("m p t -> p m t")).then_inc(rest_in, 16)
            sp.dma_start(gate[:, :, :], gate_d.rearrange("m p t -> p m t")).then_inc(rest_in, 16)

        @block.vector
        def _(dve):
            for n in range(NB):
                c = Turn(dve, dv_, n)
                yn = y[:, n, :].rearrange("p (h j) -> p h j", j=HD)
                sn = sq[:, n, :].rearrange("p (h j) -> p h j", j=HD)
                dve.wait_ge(y_in[n], 16)
                c.then("sum", dve.tensor_reduce(mean[:, n, :], yn, AX, ALU.add))
                c.then("mean", dve.tensor_scalar(mean[:, n, :], mean[:, n, :], 1.0 / HD, None, ALU.mult))
                c.mark("centre", dve.tensor_tensor(yn, yn, mean[:, n, :].unsqueeze(2).broadcast_to([P, H, HD]),
                                                   ALU.subtract))
                dve.wait_ge(ac_.sem, ac_.at(n, "square"))
                c.then("sumsq", dve.tensor_reduce(var[:, n, :], sn, AX, ALU.add))
                c.mark("var", dve.tensor_scalar(var[:, n, :], var[:, n, :], 1.0 / HD, GN_EPS, ALU.mult, ALU.add))
                dve.wait_ge(ac_.sem, ac_.at(n, "root"))
                c.then("inv", dve.reciprocal(var[:, n, :], var[:, n, :]))
                c.mark("norm", dve.tensor_tensor(yn, yn, var[:, n, :].unsqueeze(2).broadcast_to([P, H, HD]),
                                                 ALU.mult))
            for m in range(MB):
                dve.wait_ge(scaled, m + 1)
                dve.tensor_tensor(yb[:, m, :], yb[:, m, :], bonus[:, m, :], ALU.add).then_inc(out, 1)
                dve.wait_ge(out, 2 * m + 1)
                dve.tensor_tensor(yb[:, m, :], yb[:, m, :], gate[:, m, :], ALU.mult).then_inc(out, 1)

        @block.scalar
        def _(act):
            for n in range(NB):
                c = Turn(act, ac_, n)
                act.wait_ge(dv_.sem, dv_.at(n, "centre"))
                c.mark("square", act.activation(sq[:, n, :], y[:, n, :], ACT.Square))
                act.wait_ge(dv_.sem, dv_.at(n, "var"))
                c.mark("root", act.activation(var[:, n, :], var[:, n, :], ACT.Sqrt))
            act.wait_ge(rest_in, 48)
            for m in range(MB):
                act.wait_ge(turned, m + 1)
                act.activation(yb[:, m, :], ps[:, m, :], ACT.Identity, bias=col[:, 12, m:m + 1],
                               scale=col[:, 11, m:m + 1]).then_inc(scaled, 1)

        @block.tensor
        def _(pe):
            pe.wait_ge(const, 2)
            pe.wait_ge(dv_.sem, dv_.at(NB - 1, "norm"))
            for m in range(MB):
                for n in range(NB):
                    t = pe.transpose(ps[:, m, n * P:(n + 1) * P], y[:, n, m * P:(m + 1) * P], ident[:, :])
                t.then_inc(turned, 1)


def mix(nc, proj_t, at_d, yb, w_up_a, w_up_b, mixed):
    GB, GW, G = 4, 512, D // 512
    with ExitStack() as ctx:
        def sb(name, shape, dt=F32):
            return ctx.enter_context(nc.sbuf_tensor("m_" + name, shape, dt))

        sem = semaphores(nc, ctx, "m_")
        at = sb("at", [P, MB, T])
        w = [[sb(f"w{u}{s}", [P, MB, GW]) for s in range(2)] for u in range(2)]
        gt = [sb(f"gt{u}", [P, 2, GB, T]) for u in range(2)]
        other = [sb(f"other{u}", [P, T]) for u in range(2)]
        ps = ctx.enter_context(nc.psum_tensor("m_ps", [P, 8, T], F32))
        at_in = sem("at_in")
        w_in = [[sem(f"w_in{u}{s}") for s in range(2)] for u in range(2)]
        gt_in = [sem(f"gt_in{u}") for u in range(2)]
        made, opened, gated = sem("made"), sem("opened"), sem("gated")
        block = ctx.enter_context(nc.Block())
        wv = [z.rearrange("o (k p) (g c) -> g p (o k) c", p=P, c=GW) for z in (w_up_a, w_up_b)]
        gv = [proj_t[P * b:P * (b + KT)].rearrange("(g b p) t -> g p b t", p=P, b=GB) for b in (GATE_A, GATE_B)]

        @block.sync
        def _(sp):
            sp.dma_start(at[:, :, :], at_d.rearrange("m p t -> p m t")).then_inc(at_in, 16)
            for g in range(G):
                u = g % 2
                if g >= 2:
                    sp.wait_ge(made, 2 * GB * (g - 1))
                for s in range(2):
                    sp.dma_start(w[u][s][:, :, :], wv[s][g]).then_inc(w_in[u][s], 16)
                if g >= 2:
                    sp.wait_ge(gated, 3 * GB * (g - 1))
                for s in range(2):
                    sp.dma_start(gt[u][:, s, :, :], gv[s][g]).then_inc(gt_in[u], 16)

        @block.tensor
        def _(pe):
            pe.wait_ge(at_in, 16)
            for g in range(G):
                for b in range(GB):
                    j = GB * g + b
                    for s, rhs in enumerate((at, yb)):
                        pe.wait_ge(w_in[g % 2][s], 16 * (g // 2 + 1))
                        if j >= 4:
                            pe.wait_ge(gated, 3 * (j - 3))
                        for k in range(MB):
                            mm = pe.matmul(ps[:, 2 * (j % 4) + s, :], w[g % 2][s][:, k, b * P:(b + 1) * P],
                                           rhs[:, k, :], start=(k == 0), stop=(k == MB - 1))
                        mm.then_inc(made, 1)

        @block.scalar
        def _(act):
            for g in range(G):
                act.wait_ge(gt_in[g % 2], 32 * (g // 2 + 1))
                act.activation(gt[g % 2][:, :, :, :], gt[g % 2][:, :, :, :], ACT.Sigmoid).then_inc(opened, 1)

        @block.vector
        def _(dve):
            for j in range(KT):
                g, b = divmod(j, GB)
                dve.wait_ge(opened, g + 1)
                dve.wait_ge(made, 2 * j + 1)
                dve.tensor_tensor(mixed[:, j, :], ps[:, 2 * (j % 4), :], gt[g % 2][:, 0, b, :], ALU.mult)\
                   .then_inc(gated, 1)
                dve.wait_ge(made, 2 * j + 2)
                dve.tensor_tensor(other[j % 2][:, :], ps[:, 2 * (j % 4) + 1, :], gt[g % 2][:, 1, b, :], ALU.mult)\
                   .then_inc(gated, 1)
                dve.wait_ge(gated, 3 * j + 2)
                dve.tensor_tensor(mixed[:, j, :], mixed[:, j, :], other[j % 2][:, :], ALU.add).then_inc(gated, 1)


class Norm:

    def __init__(self, nc, ctx, prefix, sem):
        self.stats = [ctx.enter_context(nc.sbuf_tensor(f"{prefix}_stats{u}", [P, 4, 6], F32)) for u in range(2)]
        self.mv = [ctx.enter_context(nc.sbuf_tensor(f"{prefix}_mv{u}", [P, 2], F32)) for u in range(2)]
        self.steps = Steps(sem("norm"), 0, "stats moments eps inv centre gain shift")
        self.root = sem("root")

    def vector(self, dve, n, x, gain, shift):
        st, mv = self.stats[n % 2], self.mv[n % 2]
        c = Turn(dve, self.steps, n)
        for j in range(4):
            ins = dve.bn_stats(st[:, j, :], x[:, 512 * j:512 * (j + 1)])
        c.then("stats", ins)
        c.then("moments", dve.bn_aggr(mv[:, :], st[:, :, :].rearrange("p a b -> p (a b)")))
        c.mark("eps", dve.tensor_scalar(mv[:, 1:2], mv[:, 1:2], LN_EPS, None, ALU.add))
        dve.wait_ge(self.root, n + 1)
        c.then("inv", dve.reciprocal(mv[:, 1:2], mv[:, 1:2]))
        c.then("centre", dve.tensor_scalar(x, x, mv[:, 0:1], mv[:, 1:2], ALU.subtract, ALU.mult))
        c.then("gain", dve.tensor_tensor(x, x, gain, ALU.mult))
        c.mark("shift", dve.tensor_tensor(x, x, shift, ALU.add))

    def scalar(self, act, n):
        mv = self.mv[n % 2]
        act.wait_ge(self.steps.sem, self.steps.at(n, "eps"))
        act.activation(mv[:, 1:2], mv[:, 1:2], ACT.Sqrt).then_inc(self.root, 1)


def out_project(nc, mixed, w_o, x, ln_w, ln_b, x1_d, x1t):
    GW, G = 512, D // 512
    with ExitStack() as ctx:
        def sb(name, shape, dt=F32):
            return ctx.enter_context(nc.sbuf_tensor("o_" + name, shape, dt))

        sem = semaphores(nc, ctx, "o_")
        ident = sb("ident", [P, P])
        w = [sb(f"w{u}", [P, KT, GW]) for u in range(2)]
        res = sb("res", [P, NB, D])
        gain, shift = sb("gain", [P, D]), sb("shift", [P, D])
        norm = Norm(nc, ctx, "o", sem)
        ps = ctx.enter_context(nc.psum_tensor("o_ps", [P, 8, T], F32))
        const, x_in, ln_in = sem("const"), sem("x_in"), sem("ln_in")
        w_in = [sem(f"w_in{u}") for u in range(2)]
        made, added, turned, kept, stored = sem("made"), sem("added"), sem("turned"), sem("kept"), sem("stored")
        block = ctx.enter_context(nc.Block())
        wv = w_o.rearrange("o (k p) (g c) -> g p (o k) c", p=P, c=GW)

        @block.gpsimd
        def _(pool):
            Setup(pool, const).identity(ident)

        @block.sync
        def _(sp):
            for g in range(G):
                if g >= 2:
                    sp.wait_ge(made, NB * (g - 1))
                sp.dma_start(w[g % 2][:, :, :], wv[g]).then_inc(w_in[g % 2], 16)
                if g == 0:
                    sp.dma_start(res[:, :, :], x.rearrange("o (n p) d -> p (o n) d", p=P)).then_inc(x_in, 16)
                    sp.dma_start(gain[:, :], ln_w.partition_broadcast(P)).then_inc(ln_in, 16)
                    sp.dma_start(shift[:, :], ln_b.partition_broadcast(P)).then_inc(ln_in, 16)
            for n in range(NB):
                sp.wait_ge(norm.steps.sem, norm.steps.at(n, "shift"))
                sp.dma_start(x1_d[n * P:(n + 1) * P, :], res[:, n, :]).then_inc(stored, 16)
            sp.wait_ge(stored, 16 * NB)

        @block.tensor
        def _(pe):
            for g in range(G):
                pe.wait_ge(w_in[g % 2], 16 * (g // 2 + 1))
                for n in range(NB):
                    j = NB * g + n
                    if j >= 8:
                        pe.wait_ge(added, j - 7)
                    for k in range(KT):
                        mm = pe.matmul(ps[:, j % 8, :], mixed[:, k, n * P:(n + 1) * P], w[g % 2][:, k, :],
                                       start=(k == 0), stop=(k == KT - 1))
                    mm.then_inc(made, 1)
            pe.wait_ge(const, 2)
            pe.wait_ge(added, G * NB)
            for n in range(NB):
                pe.wait_ge(norm.steps.sem, norm.steps.at(n, "shift"))
                for k in range(0, KT, 4):
                    j = (n * KT + k) // 4
                    if j >= 8:
                        pe.wait_ge(kept, j - 7)
                    for i in range(4):
                        t = pe.transpose(ps[:, j % 8, i * P:(i + 1) * P], res[:, n, (k + i) * P:(k + i + 1) * P],
                                         ident[:, :])
                    t.then_inc(turned, 1)

        @block.scalar
        def _(act):
            norm.scalar(act, 0)
            for n in range(NB):
                if n + 1 < NB:
                    norm.scalar(act, n + 1)
                for k in range(0, KT, 4):
                    act.wait_ge(turned, (n * KT + k) // 4 + 1)
                    act.copy(x1t[:, k:k + 4, n * P:(n + 1) * P],
                             ps[:, ((n * KT + k) // 4) % 8, :].rearrange("p (i t) -> p i t", t=P)).then_inc(kept, 1)

        @block.vector
        def _(dve):
            dve.wait_ge(x_in, 16)
            for g in range(G):
                for n in range(NB):
                    j = NB * g + n
                    c = slice(GW * g, GW * (g + 1))
                    dve.wait_ge(made, j + 1)
                    dve.scalar_tensor_tensor(res[:, n, c], res[:, n, c], ALPHA, ps[:, j % 8, :],
                                             ALU.mult, ALU.add).then_inc(added, 1)
            dve.wait_ge(added, G * NB)
            dve.wait_ge(ln_in, 32)
            for n in range(NB):
                norm.vector(dve, n, res[:, n, :], gain[:, :], shift[:, :])


PH = 8
TOPK = 16
NKEY = 128
LEAST = -3.0e38
SEL = PH * TOPK


def route(nc, x1t, w_q, sub_keys, idx, gates):
    GW, G, GB = 512, D // 512, 4
    NJ = 2 * PH
    with ExitStack() as ctx:
        def sb(name, shape, dt=F32):
            return ctx.enter_context(nc.sbuf_tensor("f_" + name, shape, dt))

        sem = semaphores(nc, ctx, "f_")
        ident = sb("ident", [P, P])
        keys = sb("keys", [P, 2, P])
        keys_t = sb("keys_t", [P, 2, NKEY])
        w = [sb(f"w{u}", [P, KT, GW]) for u in range(2)]
        q = [sb(f"q{u}", [P, T]) for u in range(2)]
        s = [sb(f"s{u}", [P, NB, NKEY]) for u in range(2)]
        rest = sb("rest", [P, NB, NKEY])
        top = sb("top", [P, NB, NJ, TOPK])
        top_i = sb("top_i", [P, NB, NJ, TOPK], U32)
        top_f = sb("top_f", [P, NB, NJ, TOPK])
        cand = [sb(f"cand{u}", [P, PH, TOPK * TOPK]) for u in range(2)]
        best = sb("best", [P, NB, PH, TOPK])
        pos = sb("pos", [P, NB, PH, TOPK], U32)
        half = sb("half", [P, 2, PH, TOPK], U32)
        half_f = sb("half_f", [P, 2, PH, TOPK])
        iota = sb("iota", [P, TOPK], mybir.dt.int32)
        iota_f = sb("iota_f", [P, TOPK])
        match = [sb(f"match{u}", [P, SEL, TOPK]) for u in range(2)]
        found = sb("found", [P, 2, SEL])
        total = sb("total", [P, NB, PH])
        ps = ctx.enter_context(nc.psum_tensor("f_ps", [P, 8, T], F32))
        const, keys_in, keys_turned, keys_kept = sem("const"), sem("keys_in"), sem("keys_turned"), sem("keys_kept")
        w_in = [sem(f"w_in{u}") for u in range(2)]
        q_made, q_kept, s_made, s_kept = sem("q_made"), sem("q_kept"), sem("s_made"), sem("s_kept")
        tk = Steps(sem("tk"), 1, "max0 index0 rest max1 index1")
        cn = Steps(sem("cn"), tk.end(NJ) + 1,
                   "cand max0 index0 rest max1 index1 shift mask float match0 match1 pick0 pick1 sum0 sum1 index")
        cn.sem = tk.sem
        sm = Steps(tk.sem, cn.end(NB), "less sum inverse gate")
        exped = sem("exped")
        block = ctx.enter_context(nc.Block())
        wv = w_q.rearrange("o (k p) (g c) -> g p (o k) c", p=P, c=GW)

        @block.gpsimd
        def _(pool):
            c = Setup(pool, const)
            c.identity(ident)
            c.step(pool.iota(iota[:, :], pattern=[[1, TOPK]], base=0, channel_multiplier=0))
            assert c.n == 3

        @block.sync
        def _(sp):
            sp.dma_start(keys[:, :, :], sub_keys.rearrange("o c n d -> n (o c) d")).then_inc(keys_in, 16)
            for g in range(G):
                if g >= 2:
                    sp.wait_ge(q_made, GB * (g - 1))
                sp.dma_start(w[g % 2][:, :, :], wv[g]).then_inc(w_in[g % 2], 16)

        @block.tensor
        def _(pe):
            pe.wait_ge(const, 2)
            pe.wait_ge(keys_in, 16)
            for c in range(2):
                t = pe.transpose(ps[:, 7, c * P:(c + 1) * P], keys[:, c, :], ident[:, :])
            t.then_inc(keys_turned, 1)

            def scores(j):
                pe.wait_ge(q_kept, j + 1)
                if j == 0:
                    pe.wait_ge(keys_kept, 1)
                if j >= 4:
                    pe.wait_ge(s_kept, j - 3)
                for n in range(NB):
                    mm = pe.matmul(ps[:, 4 + j % 4, n * P:(n + 1) * P], q[j % 2][:, n * P:(n + 1) * P],
                                   keys_t[:, j % 2, :], start=True, stop=True)
                mm.then_inc(s_made, 1)
            for j in range(NJ):
                g, b = divmod(j, GB)
                pe.wait_ge(w_in[g % 2], 16 * (g // 2 + 1))
                if j >= 4:
                    pe.wait_ge(q_kept, j - 3)
                for k in range(KT):
                    mm = pe.matmul(ps[:, j % 4, :], w[g % 2][:, k, b * P:(b + 1) * P], x1t[:, k, :],
                                   start=(k == 0), stop=(k == KT - 1))
                mm.then_inc(q_made, 1)
                if j >= 1:
                    scores(j - 1)
            scores(NJ - 1)

        @block.scalar
        def _(act):
            act.wait_ge(keys_turned, 1)
            act.copy(keys_t[:, :, :].rearrange("p c n -> p (c n)"), ps[:, 7, 0:2 * P]).then_inc(keys_kept, 1)
            for j in range(NJ + 1):
                if j < NJ:
                    act.wait_ge(q_made, j + 1)
                    if j >= 2:
                        act.wait_ge(s_made, j - 1)
                    act.copy(q[j % 2][:, :], ps[:, j % 4, :]).then_inc(q_kept, 1)
                if j >= 1:
                    act.wait_ge(s_made, j)
                    if j >= 3:
                        act.wait_ge(tk.sem, tk.at(j - 3, "rest"))
                    act.copy(s[(j - 1) % 2][:, :, :].rearrange("p n k -> p (n k)"), ps[:, 4 + (j - 1) % 4, :])\
                       .then_inc(s_kept, 1)
            act.wait_ge(sm.sem, sm.at(0, "less"))
            flat = best[:, :, :, :].rearrange("p n h k -> p (n h k)")
            act.activation(flat, flat, ACT.Exp).then_inc(exped, 1)

        @block.vector
        def _(dve):
            dve.wait_ge(const, 3)
            dve.tensor_copy(iota_f[:, :], iota[:, :]).then_inc(tk.sem, 1)

            def top16(c, keys_of, rest_of, out, out_i, count):
                def each(name, make, wait=True):
                    for n in range(count):
                        ins = make(n)
                    (c.then if wait else c.mark)(name, ins)
                each("max0", lambda n: dve.max(out(n)[:, 0:8], keys_of(n)))
                each("index0", lambda n: dve.max_index(out_i(n)[:, 0:8], out(n)[:, 0:8], keys_of(n)), False)
                each("rest", lambda n: dve.match_replace(rest_of(n), out(n)[:, 0:8], keys_of(n), LEAST))
                each("max1", lambda n: dve.max(out(n)[:, 8:16], rest_of(n)))
                each("index1", lambda n: dve.max_index(out_i(n)[:, 8:16], out(n)[:, 8:16], rest_of(n)))
            for j in range(NJ):
                c = Turn(dve, tk, j)
                dve.wait_ge(s_kept, j + 1)
                top16(c, lambda n: s[j % 2][:, n, :], lambda n: rest[:, n, :], lambda n: top[:, n, j, :],
                      lambda n: top_i[:, n, j, :], NB)
            dve.tensor_copy(top_f[:, :, :, :].rearrange("p n j k -> p (n j k)"),
                            top_i[:, :, :, :].rearrange("p n j k -> p (n j k)")).then_inc(tk.sem, 1)
            for n in range(NB):
                c = Turn(dve, cn, n)
                two = top[:, n, :, :].rearrange("p (h c) k -> p h c k", c=2)
                names = top_f[:, n, :, :].rearrange("p (h c) k -> p h c k", c=2)
                wide = [P, PH, TOPK, TOPK]
                c.then("cand", dve.tensor_tensor(
                    cand[0][:, :, :].rearrange("p h (a b) -> p h a b", b=TOPK),
                    two[:, :, 0, :].unsqueeze(3).broadcast_to(wide), two[:, :, 1, :].unsqueeze(2).broadcast_to(wide),
                    ALU.add))
                top16(c, lambda h: cand[0][:, h, :], lambda h: cand[1][:, h, :], lambda h: best[:, n, h, :],
                      lambda h: pos[:, n, h, :], PH)
                c.mark("shift", dve.tensor_scalar(half[:, 0, :, :], pos[:, n, :, :], 4, None, ALU.logical_shift_right))
                c.then("mask", dve.tensor_scalar(half[:, 1, :, :], pos[:, n, :, :], 15, None, ALU.bitwise_and))
                c.then("float", dve.tensor_copy(half_f[:, :, :, :].rearrange("p c h k -> p (c h k)"),
                                                half[:, :, :, :].rearrange("p c h k -> p (c h k)")))
                for i in range(2):
                    ins = dve.tensor_tensor(
                        match[i][:, :, :], half_f[:, i, :, :].rearrange("p h k -> p (h k)").unsqueeze(2)
                        .broadcast_to([P, SEL, TOPK]), iota_f[:, :].unsqueeze(1).broadcast_to([P, SEL, TOPK]),
                        ALU.is_equal)
                    c.mark(f"match{i}", ins)
                dve.wait_ge(cn.sem, cn.at(n, "match1"))
                for i in range(2):
                    m4 = match[i][:, :, :].rearrange("p (h k) a -> p h k a", k=TOPK)
                    c.mark(f"pick{i}", dve.tensor_tensor(
                        m4, m4, names[:, :, i, :].unsqueeze(2).broadcast_to(wide), ALU.mult))
                dve.wait_ge(cn.sem, cn.at(n, "pick1"))
                for i in range(2):
                    c.mark(f"sum{i}", dve.tensor_reduce(found[:, i, :], match[i][:, :, :], AX, ALU.add))
                dve.wait_ge(cn.sem, cn.at(n, "sum1"))
                c.then("index", dve.scalar_tensor_tensor(idx[:, n, :], found[:, 0, :], float(NKEY), found[:, 1, :],
                                                         ALU.mult, ALU.add))
            c = Turn(dve, sm, 0)
            b3 = best[:, :, :, :].rearrange("p n h k -> p (n h) k")
            wide = [P, NB * PH, TOPK]
            for_max = total[:, :, :].rearrange("p n h -> p (n h)")
            dve.tensor_copy(for_max, b3[:, :, 0]).then_inc(exped, 1)
            dve.wait_ge(exped, 1)
            c.mark("less", dve.tensor_tensor(b3, b3, for_max.unsqueeze(2).broadcast_to(wide), ALU.subtract))
            dve.wait_ge(exped, 2)
            c.then("sum", dve.tensor_reduce(for_max, b3, AX, ALU.add))
            c.then("inverse", dve.reciprocal(for_max, for_max))
            c.mark("gate", dve.tensor_tensor(gates[:, :, :].rearrange("p n (h k) -> p (n h) k", k=TOPK), b3,
                                             for_max.unsqueeze(2).broadcast_to(wide), ALU.mult))


def per_layer_embedding(nc, x1t, p_in, w_gate, w_proj, ple_d):
    GW, G, PD = 512, D // 512, 256
    KP = PD // P
    with ExitStack() as ctx:
        def sb(name, shape, dt=F32):
            return ctx.enter_context(nc.sbuf_tensor("g_" + name, shape, dt))

        sem = semaphores(nc, ctx, "g_")
        ident = sb("ident", [P, P])
        pin = sb("pin", [P, NB, PD])
        pt = sb("pt", [P, KP, T])
        wp = sb("wp", [P, KP, D])
        w = [sb(f"w{u}", [P, KT, GW]) for u in range(2)]
        sg = [sb(f"sg{u}", [P, GW]) for u in range(2)]
        out = [sb(f"out{u}", [P, GW]) for u in range(2)]
        ps = ctx.enter_context(nc.psum_tensor("g_ps", [P, 8, T], F32))
        const, p_loaded, wp_in = sem("const"), sem("p_loaded"), sem("wp_in")
        w_in = [sem(f"w_in{u}") for u in range(2)]
        p_turned, p_kept, made, opened, product = (sem(n) for n in ("p_turned", "p_kept", "made", "opened", "product"))
        stored = [sem(f"stored{u}") for u in range(2)]
        block = ctx.enter_context(nc.Block())
        wv = w_gate.rearrange("o (k p) (g c) -> g p (o k) c", p=P, c=GW)

        @block.gpsimd
        def _(pool):
            Setup(pool, const).identity(ident)

        @block.sync
        def _(sp):
            sp.dma_start(pin[:, :, :], p_in.rearrange("o q (n p) d -> p (o q n) d", p=P)).then_inc(p_loaded, 16)
            sp.dma_start(w[0][:, :, :], wv[0]).then_inc(w_in[0], 16)
            sp.dma_start(wp[:, :, :], w_proj.rearrange("o (k p) d -> p (o k) d", p=P)).then_inc(wp_in, 16)
            sp.dma_start(w[1][:, :, :], wv[1]).then_inc(w_in[1], 16)
            for g in range(G):
                for n in range(NB):
                    j = g * NB + n
                    sp.wait_ge(product, j + 1)
                    sp.dma_start(ple_d[n * P:(n + 1) * P, g * GW:(g + 1) * GW], out[j % 2][:, :])\
                      .then_inc(stored[j % 2], 16)
                if g + 2 < G:
                    sp.dma_start(w[g % 2][:, :, :], wv[g + 2]).then_inc(w_in[g % 2], 16)
            for u in range(2):
                sp.wait_ge(stored[u], 16 * G * NB // 2)

        @block.tensor
        def _(pe):
            pe.wait_ge(const, 2)
            pe.wait_ge(p_loaded, 16)
            for k in range(KP):
                for n in range(NB):
                    t = pe.transpose(ps[:, 6 + k, n * P:(n + 1) * P], pin[:, n, k * P:(k + 1) * P], ident[:, :])
                t.then_inc(p_turned, 1)
            pe.wait_ge(p_kept, KP)
            for g in range(G):
                pe.wait_ge(w_in[g % 2], 16 * (g // 2 + 1))
                pe.wait_ge(wp_in, 16)
                for n in range(NB):
                    j = g * NB + n
                    if j >= 4:
                        pe.wait_ge(product, j - 3)
                    for k in range(KT):
                        mm = pe.matmul(ps[:, j % 4, :], x1t[:, k, n * P:(n + 1) * P], w[g % 2][:, k, :],
                                       start=(k == 0), stop=(k == KT - 1))
                    for k in range(KP):
                        mm = pe.matmul(ps[:, 4 + j % 4, :], pt[:, k, n * P:(n + 1) * P],
                                       wp[:, k, g * GW:(g + 1) * GW], start=(k == 0), stop=(k == KP - 1))
                    mm.then_inc(made, 1)

        @block.scalar
        def _(act):
            for k in range(KP):
                act.wait_ge(p_turned, k + 1)
                act.copy(pt[:, k, :], ps[:, 6 + k, :]).then_inc(p_kept, 1)
            for j in range(G * NB):
                act.wait_ge(made, j + 1)
                if j >= 2:
                    act.wait_ge(product, j - 1)
                act.activation(sg[j % 2][:, :], ps[:, j % 4, :], ACT.Sigmoid).then_inc(opened, 1)

        @block.vector
        def _(dve):
            for j in range(G * NB):
                dve.wait_ge(opened, j + 1)
                if j >= 2:
                    dve.wait_ge(stored[j % 2], 16 * (j // 2))
                dve.tensor_tensor(out[j % 2][:, :], sg[j % 2][:, :], ps[:, 4 + j % 4, :], ALU.mult)\
                   .then_inc(product, 1)


def experts(nc, x1_d, ple_d, idx, gates, expert_u, expert_v, ln_w, ln_b, out_d):
    RING = 8
    TURNS = SEL // RING
    with ExitStack() as ctx:
        def sb(name, shape, dt=F32):
            return ctx.enter_context(nc.sbuf_tensor("h_" + name, shape, dt))

        sem = semaphores(nc, ctx, "h_")
        u_rows = [sb(f"u{r}", [P, D]) for r in range(RING)]
        v_rows = [sb(f"v{r}", [P, D]) for r in range(RING)]
        x1 = sb("x1", [P, D])
        ple = sb("ple", [P, D])
        y = [sb(f"y{r}", [P, D]) for r in range(2)]
        gain, shift = sb("gain", [P, D]), sb("shift", [P, D])
        idx_now = [sb(f"idx_now{r}", [P, RING], U32) for r in range(2)]
        dots = sb("dots", [P, RING])
        acts = sb("acts", [P, RING])
        norm = Norm(nc, ctx, "h", sem)
        ln_in, x_in, stored, seq, cleared = sem("ln_in"), sem("x_in"), sem("stored"), sem("seq"), sem("cleared")
        u_in = [sem(f"u_in{r}") for r in range(RING)]
        v_in = [sem(f"v_in{r}") for r in range(RING)]
        idx_ready, dotted, gelu_done, act_done, added, summed = (
            sem(n) for n in ("idx_ready", "dotted", "gelu_done", "act_done", "added", "summed"))
        block = ctx.enter_context(nc.Block())
        uv_, vv_ = expert_u.rearrange("o e d -> (o e) d"), expert_v.rearrange("o e d -> (o e) d")

        @block.sync
        def _(sp):
            sp.dma_start(gain[:, :], ln_w.partition_broadcast(P)).then_inc(ln_in, 16)
            sp.dma_start(shift[:, :], ln_b.partition_broadcast(P)).then_inc(ln_in, 16)
            for n in range(NB):
                if n >= 1:
                    sp.wait_ge(summed, 4 * n)
                sp.dma_start(x1[:, :], x1_d[n * P:(n + 1) * P, :]).then_inc(x_in, 16)
                sp.dma_start(ple[:, :], ple_d[n * P:(n + 1) * P, :]).then_inc(x_in, 16)
                sp.wait_ge(norm.steps.sem, norm.steps.at(n, "shift"))
                sp.dma_start(out_d[0, n * P:(n + 1) * P, :], y[0][:, :]).then_inc(stored, 16)
            sp.wait_ge(stored, 16 * NB)

        @block.gpsimd
        def _(pool):
            for n in range(NB):
                with pool.Fori(0, TURNS // 2) as i:
                    for b in range(2):
                        t = i * 2 + (n * TURNS + b)
                        pool.wait_ge(idx_ready, t + 1)
                        pool.sem_inc(seq, 1)
                        for ready, rows, table, slots in ((dotted, u_rows, uv_, u_in), (added, v_rows, vv_, v_in)):
                            for r in range(RING):
                                pool.wait_ge(ready, t * RING + (r + 2))
                                pool.sem_inc(seq, 1)
                                pool.indirect_dma_start(
                                    rows[r][:, :], None, table,
                                    bass.IndirectOffsetOnAxis(ap=idx_now[b][:, r:r + 1], axis=0)).then_inc(slots[r], 16)

        @block.scalar
        def _(act):
            for n in range(NB):
                with act.Fori(0, TURNS // 2) as i:
                    for b in range(2):
                        t = i * 2 + (n * TURNS + b)
                        act.wait_ge(added, t * RING + 1)
                        act.copy(idx_now[b][:, :], idx[:, n, bass.ds(i * (2 * RING) + b * RING, RING)])\
                           .then_inc(idx_ready, 1)
                        act.wait_ge(dotted, (t + 2) * RING + 1)
                        act.activation(acts[:, :], dots[:, :], ACT.Gelu).then_inc(gelu_done, 1)
                norm.scalar(act, n)

        @block.vector
        def _(dve):
            dve.sem_inc(dotted, RING + 1)
            dve.sem_inc(added, RING + 1)
            dve.sem_inc(act_done, 1)
            for n in range(NB):
                if n >= 1:
                    dve.wait_ge(stored, 16 * n)
                for r in range(2):
                    dve.memset(y[r][:, :], 0.0).then_inc(cleared, 1)
                dve.wait_ge(x_in, 32 * (n + 1))
                dve.wait_ge(cleared, 2 * (n + 1))
                with dve.Fori(0, TURNS) as i:
                    t = i + n * TURNS
                    for r in range(RING):
                        dve.wait_ge(u_in[r], t * 16 + 16)
                        if r == 0:
                            dve.wait_ge(act_done, t + 1)
                        dve.tensor_tensor_reduce(u_rows[r][:, :], u_rows[r][:, :], x1[:, :], 1.0, 0.0, ALU.mult, ALU.add,
                                                 dots[:, r:r + 1]).then_inc(dotted, 1)
                    dve.wait_ge(gelu_done, t + 1)
                    dve.tensor_tensor(acts[:, :], acts[:, :], gates[:, n, bass.ds(i * RING, RING)], ALU.mult)\
                       .then_inc(act_done, 1)
                    dve.wait_ge(act_done, t + 2)
                    for r in range(RING):
                        dve.wait_ge(v_in[r], t * 16 + 16)
                        dve.wait_ge(added, t * RING + (r + 8))
                        dve.scalar_tensor_tensor(y[r % 2][:, :], v_rows[r][:, :], acts[:, r:r + 1], y[r % 2][:, :],
                                                 ALU.mult, ALU.add).then_inc(added, 1)
                dve.wait_ge(added, RING * (TURNS * (n + 1) + 1) + 1)
                dve.tensor_tensor(y[0][:, :], y[0][:, :], y[1][:, :], ALU.add).then_inc(summed, 1)
                dve.wait_ge(summed, 4 * n + 1)
                dve.scalar_tensor_tensor(y[0][:, :], x1[:, :], ALPHA, y[0][:, :], ALU.mult, ALU.add)\
                   .then_inc(summed, 1)
                dve.wait_ge(summed, 4 * n + 2)
                dve.tensor_tensor(y[0][:, :], y[0][:, :], ple[:, :], ALU.add).then_inc(summed, 2)
                dve.wait_ge(summed, 4 * n + 4)
                if n == 0:
                    dve.wait_ge(ln_in, 32)
                norm.vector(dve, n, y[0][:, :], gain[:, :], shift[:, :])


def build(nc, a, out):
    def dram(name, shape):
        return nc.dram_tensor(name, shape, F32, kind="Internal").ap()
    proj_t = dram("proj_t", [IN_COLS, T])
    ar_d, bk_t_d = dram("ar_d", [NC, P, MB, 2 * L]), dram("bk_t_d", [NC, P, MB, P])
    g_d, v_d = dram("g_d", [NC, P, H, 2 * L]), dram("v_d", [NC, L, MB, P])
    bonus_d, gate_d = dram("bonus_d", [MB, P, T]), dram("gate_d", [MB, P, T])
    cols_d, decay_d = dram("cols_d", [P, 6 + len(PARAMS), MB]), dram("decay_d", [P, MB, NC])
    wt_d, y_d, at_d = dram("wt_d", [NC, L, H, L]), dram("y_d", [T, W]), dram("at_d", [MB, P, T])
    x1_d, ple_d = dram("x1_d", [T, D]), dram("ple_d", [T, D])
    vecs = [a[n].rearrange("o (m e) j -> (o m) (e j)", e=2) if n == "rwkv_r_k" else
            a[n].rearrange("o (m p) -> (o m) p", p=P) for n in PARAMS]

    project_in(nc, a["x"], a["w_in"], proj_t)
    rwkv_prepare(nc, proj_t, a["rwkv_mu"], vecs, a["rwkv_w_lora1"], a["rwkv_w_lora2"], a["rwkv_a_lora1"],
                 a["rwkv_a_lora2"], a["rwkv_g_lora1"], a["rwkv_g_lora2"],
                 ar_d, bk_t_d, g_d, v_d, bonus_d, gate_d, cols_d, decay_d)
    rwkv_invert(nc, g_d, wt_d)
    rwkv_scan(nc, ar_d, bk_t_d, g_d, v_d, decay_d, wt_d, y_d)
    attention(nc, proj_t, at_d)
    with ExitStack() as ctx:
        idx = ctx.enter_context(nc.sbuf_tensor("idx", [P, NB, SEL], U32))
        gates = ctx.enter_context(nc.sbuf_tensor("gates", [P, NB, SEL], F32))
        with nc.sbuf_tensor("x1t", [P, KT, T], F32) as x1t:
            with nc.sbuf_tensor("mixed", [P, KT, T], F32) as mixed:
                with nc.sbuf_tensor("yb", [P, MB, T], F32) as yb:
                    rwkv_finish(nc, y_d, cols_d, bonus_d, gate_d, yb)
                    mix(nc, proj_t, at_d, yb, a["w_up_a"], a["w_up_b"], mixed)
                out_project(nc, mixed, a["w_o"], a["x"], a["ln1_w"], a["ln1_b"], x1_d, x1t)
            route(nc, x1t, a["peer_w_q"], a["peer_sub_keys"], idx, gates)
            per_layer_embedding(nc, x1t, a["p"], a["ple_w_gate"], a["ple_w_proj"], ple_d)
        experts(nc, x1_d, ple_d, idx, gates, a["peer_u"], a["peer_v"], a["ln2_w"], a["ln2_b"], out)


INPUTS = ["x", "p", "w_in", "rwkv_mu", "rwkv_w0", "rwkv_w_lora1", "rwkv_w_lora2", "rwkv_a0", "rwkv_a_lora1",
          "rwkv_a_lora2", "rwkv_g_lora1", "rwkv_g_lora2", "rwkv_k_k", "rwkv_k_a", "rwkv_r_k", "rwkv_lnx_w",
          "rwkv_lnx_b", "w_up_a", "w_up_b", "w_o", "ln1_w", "ln1_b", "peer_w_q", "peer_sub_keys", "peer_u",
          "peer_v", "ple_w_gate", "ple_w_proj", "ln2_w", "ln2_b"]


def kernel(**inputs):
    import numpy as np
    import concourse.bacc as bacc
    from concourse.bass_utils import run_bass_kernel_spmd

    nc = bacc.Bacc("TRN2", target_bir_lowering=False, num_devices=1)
    arrays, a = {}, {}
    for name in INPUTS:
        arrays[f"in_{name}"] = np.ascontiguousarray(inputs[name])
        a[name] = nc.dram_tensor(f"in_{name}", arrays[f"in_{name}"].shape, F32, kind="ExternalInput").ap()
    out = nc.dram_tensor("out", (1, T, D), F32, kind="ExternalOutput").ap()
    build(nc, a, out)
    return run_bass_kernel_spmd(nc, [arrays], core_ids=[0]).results[0]["out"]
```

```python
import math
from contextlib import ExitStack
import concourse.bass as bass
from concourse import mybir

P = 128
T = 512
D = 2048
KT = D // P
NB = T // P
IN_COLS = 11264
F32 = mybir.dt.float32
F32R = mybir.dt.float32r
U32 = mybir.dt.uint32
ALU = mybir.AluOpType
ACT = mybir.ActivationFunctionType
AX = mybir.AxisListType.X


def semaphores(nc, ctx, prefix):
    made = []

    def sem(name):
        made.append(nc.alloc_semaphore(prefix + name))
        return made[-1]

    def give_back():
        nc.clear_and_free_semaphores(made)
        nc.all_engine_barrier()
    ctx.callback(give_back)
    return sem


class Steps:

    def __init__(self, eng_sem, first, names):
        self.sem, self.first, self.names = eng_sem, first, names.split()

    def at(self, turn, name):
        return turn * len(self.names) + (self.first + self.names.index(name) + 1)

    def end(self, turns):
        return self.first + turns * len(self.names)


class Turn:

    def __init__(self, eng, steps, turn):
        self.eng, self.steps, self.turn, self.n = eng, steps, turn, 0

    def mark(self, name, ins):
        assert self.steps.names[self.n] == name, (self.steps.names[self.n], name)
        self.n += 1
        return ins.then_inc(self.steps.sem, 1)

    def then(self, name, ins):
        self.mark(name, ins)
        self.eng.wait_ge(self.steps.sem, self.steps.at(self.turn, name))


class Setup:

    def __init__(self, pool, sem):
        self.pool, self.sem, self.n = pool, sem, 0

    def step(self, ins):
        self.n += 1
        ins.then_inc(self.sem, 1)
        self.pool.wait_ge(self.sem, self.n)

    def fill(self, tile, value):
        self.step(self.pool.memset(tile, value))

    def keep(self, tile, op, pattern, channel, fill, base=0):
        self.step(self.pool.affine_select(out=tile, in_=tile, compare_op=op, fill=fill, base=base,
                                          pattern=pattern, channel_multiplier=channel))

    def identity(self, ident):
        self.fill(ident[:, :], 0.0)
        self.keep(ident[:, :], ALU.not_equal, [[-1, P]], 1, 1.0)


def split(act, dve, part, whole, hi, lo, done):
    if part == "hi":
        return act.activation(hi, whole, ACT.Copy).then_inc(done, 1)
    return dve.tensor_tensor(lo, whole, hi.bitcast(F32), ALU.subtract).then_inc(done, 1)


def product(pe, out, lhs, rhs, first, last):
    for n, (a, b) in enumerate(((0, 0), (0, 1), (1, 0))):
        mm = pe.matmul(out, lhs[a], rhs[b], start=(first and n == 0), stop=(last and n == 2))
    return mm


def project_in(nc, x, w_in, proj_t):
    GW = 256
    NQ = IN_COLS // P
    xv = x.rearrange("o (n p) d -> p (o n) d", p=P)
    wv = w_in.rearrange("o (k p) (g c) -> g p (o k) c", p=P, c=GW)
    ov = proj_t.rearrange("(g b p) t -> g p b t", b=2, p=P)
    with ExitStack() as ctx:
        sem = semaphores(nc, ctx, "a_")

        def sb(name, shape, dt=F32):
            return ctx.enter_context(nc.sbuf_tensor("a_" + name, shape, dt))
        ident = sb("ident", [P, P])
        xt = [sb(f"xt{s}", [P, KT, T], F32R) for s in range(2)]
        xin = sb("xin", [P, NB, D])
        raw = [sb(f"raw{u}", [P, KT, GW]) for u in range(2)]
        w = [[sb(f"w{s}{r}", [P, KT, P], F32R) for r in range(4)] for s in range(2)]
        ob = [sb(f"ob{u}", [P, 2, T]) for u in range(2)]
        ps = ctx.enter_context(nc.psum_tensor("a_ps", [P, 8, T], F32))
        ident_done = sem("ident_done")
        x_in = [sem(f"x_in{n}") for n in range(NB)]
        x_turned, xt_hi, xt_lo = sem("x_turned"), sem("xt_hi"), sem("xt_lo")
        raw_in = [sem(f"raw_in{u}") for u in range(2)]
        hi_done, lo_done, blocks_done = sem("hi_done"), sem("lo_done"), sem("blocks_done")
        out_done = [sem("out_act"), sem("out_dve")]
        stored = [sem(f"stored{u}") for u in range(2)]
        block = ctx.enter_context(nc.Block())

        def looped(eng, before, step):
            before()
            with eng.Fori(0, NQ // 4 - 1) as i:
                for s in range(4):
                    step(i * 4 + s, i, s, True)
            for s in range(4):
                step(NQ - 4 + s, NQ // 4 - 1, s, s < 2)

        @block.gpsimd
        def _(pool):
            Setup(pool, ident_done).identity(ident)

        @block.sync
        def _(sp):
            for n in range(NB):
                sp.dma_start(xin[:, n, :], xv[:, n, :]).then_inc(x_in[n], 16)
            for u in range(2):
                sp.sem_inc(stored[u], 16)
                sp.dma_start(raw[u][:, :, :], wv[u]).then_inc(raw_in[u], 16)

            def store(g, u, dst):
                for o in out_done:
                    sp.wait_ge(o, g + 3)
                sp.dma_start(dst, ob[u][:, :, :]).then_inc(stored[u], 16)
            with sp.Fori(0, NQ // 4 - 1) as i:
                for u in range(2):
                    sp.wait_ge(lo_done, i * 4 + (2 * u + 2))
                    sp.dma_start(raw[u][:, :, :], wv[bass.ds(i * 2 + (2 + u), 1)].rearrange("g p k c -> (g p) k c"))\
                      .then_inc(raw_in[u], 16)
                for u in range(2):
                    store(i * 2 + u, u, ov[bass.ds(i * 2 + u, 1)].rearrange("g p b t -> (g p) b t"))
            for u in range(2):
                store(NQ // 2 - 2 + u, u, ov[NQ // 2 - 2 + u])
            for u in range(2):
                sp.wait_ge(stored[u], 16 * (NQ // 4) + 16)

        @block.tensor
        def _(pe):
            pe.wait_ge(ident_done, 2)
            for n in range(NB):
                pe.wait_ge(x_in[n], 16)
            for k in range(KT):
                if k >= 8:
                    pe.wait_ge(xt_lo, k - 7)
                for n in range(NB):
                    t = pe.transpose(ps[:, k % 8, n * P:(n + 1) * P], xin[:, n, k * P:(k + 1) * P], ident[:, :])
                t.then_inc(x_turned, 1)
            pe.wait_ge(xt_lo, KT)

            def step(q, i, s, more):
                pe.wait_ge(lo_done, q + 1)
                pe.wait_ge(out_done[s % 2], i * 2 + (s // 2 + 1))
                for k in range(KT):
                    mm = product(pe, ps[:, s, :], [w[h][s][:, k, :] for h in range(2)],
                                 [xt[h][:, k, :] for h in range(2)], k == 0, k == KT - 1)
                mm.then_inc(blocks_done, 1)
            looped(pe, lambda: pe.sem_inc(blocks_done, 4), step)

        def halves(eng, part, copy, done):
            odd = part == "lo"

            def part_of(q, i, s):
                u, b = s // 2, s % 2
                eng.wait_ge(raw_in[u], i * 16 + 16)
                if odd:
                    eng.wait_ge(hi_done, q + 1)
                eng.wait_ge(blocks_done, q + 1)
                split(nc.scalar, nc.vector, part, raw[u][:, :, b * P:(b + 1) * P], w[0][s][:, :, :], w[1][s][:, :, :],
                      done)

            def before():
                eng.sem_inc(out_done[odd], 2)
                for k in range(KT):
                    eng.wait_ge(x_turned, k + 1)
                    if odd:
                        eng.wait_ge(xt_hi, k + 1)
                    split(nc.scalar, nc.vector, part, ps[:, k % 8, :], xt[0][:, k, :], xt[1][:, k, :],
                          xt_lo if odd else xt_hi)
                part_of(0, 0, 0)
                part_of(1, 0, 1)

            def step(q, i, s, more):
                if more:
                    part_of(q + 2, i + (s + 2) // 4, (s + 2) % 4)
                if s % 2 == odd:
                    eng.wait_ge(stored[s // 2], i * 16 + 16)
                    eng.wait_ge(blocks_done, q + 5)
                    copy(ob[s // 2][:, s % 2, :], ps[:, s, :]).then_inc(out_done[odd], 1)
            looped(eng, before, step)

        @block.scalar
        def _(act):
            halves(act, "hi", nc.scalar.copy, hi_done)

        @block.vector
        def _(dve):
            halves(dve, "lo", nc.vector.tensor_copy, lo_done)


L = 64
NC = T // L
HD = 64
W = 1024
MB = W // P
H = W // HD
OFF_R = 3 * W
PARAMS = ["rwkv_w0", "rwkv_a0", "rwkv_k_k", "rwkv_k_a", "rwkv_r_k", "rwkv_lnx_w", "rwkv_lnx_b"]
DECAY = -math.exp(-0.5)


def rwkv_prepare(nc, proj_t, rwkv_mu, vecs, w_lora1, w_lora2, a_lora1, a_lora2, g_lora1, g_lora2,
                 ar_d, bk_t_d, g_d, v_d, bonus_d, gate_d, cols_d, decay_d):
    pv = proj_t.rearrange("(b p) t -> b p t", p=P)
    R0, K0, V0, C0 = (OFF_R // P + i * MB for i in range(4))
    with ExitStack() as ctx:
        def sb(name, shape, dt=F32):
            return ctx.enter_context(nc.sbuf_tensor("b_" + name, shape, dt))

        sem = semaphores(nc, ctx, "b_")
        ident = sb("ident", [P, P])
        ones = sb("ones", [P, P])
        mask = sb("mask", [P, 2, L])
        restart = sb("restart", [P, NC, L])
        rows = sb("rows", [(6 + len(PARAMS)) * MB, P])
        col = sb("col", [P, 6 + len(PARAMS), MB])
        ka1 = sb("ka1", [P, MB])
        w1 = sb("w1", [P, MB, 64])
        a1 = sb("a1", [P, MB, 64])
        g1 = sb("g1", [P, MB, 160])
        w2 = sb("w2", [64, W])
        a2 = sb("a2", [64, W])
        g2a = sb("g2a", [P, W])
        g2b = sb("g2b", [32, W])
        hw = sb("hw", [64, T])
        ha = sb("ha", [64, T])
        hga = sb("hga", [P, T])
        hgb = sb("hgb", [32, T])
        zin = sb("zin", [P, 2, 3, T + 1])
        dif = sb("dif", [P, 3, T])
        x3 = sb("x3", [P, 2, 3, T])
        r, k, v = (sb(n, [P, T]) for n in "rkv")
        sw, av, lw, cum, cumx = (sb(n, [P, T]) for n in ("sw", "av", "lw", "cum", "cumx"))
        e_in, e_out, e_prev = (sb(n, [P, T]) for n in ("e_in", "e_out", "e_prev"))
        kk, sq, nrm, k2, tmp, bon = (sb(n, [P, T]) for n in ("kk", "sq", "nrm", "k2", "tmp", "bon"))
        gs = sb("gs", [P, T])
        ar = sb("ar", [P, NC, 2, L])
        bk = sb("bk", [P, NC, 2, L])
        gm = sb("gm", [P, NC, 2, 2 * L])
        bkt = sb("bkt", [P, NC, P])
        vt = sb("vt", [L, NC, P])
        dec = sb("dec", [P, MB, NC])
        ps = ctx.enter_context(nc.psum_tensor("b_ps", [P, 8, T], F32))
        s = {n: sem(n) for n in (
            "const", "rows_in", "wl_in", "pe", "act", "dve", "st_g", "st_ar", "st_gm", "st_bkt", "st_vt", "st_bon", "st_end")}
        c_in = [sem(f"c_in{u}") for u in range(2)]
        z_in = [sem(f"z_in{u}") for u in range(2)]
        block = ctx.enter_context(nc.Block())
        NV = 6 + len(PARAMS)
        PE0, AC0, DV0 = 1, 1, 1
        p1pe = Steps(s["pe"], PE0, "lora")
        p1dve = Steps(s["dve"], DV0, "diff shift")
        AC1 = AC0 + 4
        pe_ = Steps(s["pe"], p1pe.end(MB), "decay_in rate_in gate_in square_sum bonus_sum chunks bk_turned v_turned")
        ac_ = Steps(s["act"], AC1, "decay_sig rate log_decay square gate norm e_in e_out e_prev bk_copied v_copied")
        dv_ = Steps(s["dve"], p1dve.end(MB),
                    "diff shift kk_raw cum cum_prev k_part k_new norm_max norm_inv kk kk_a rk_part "
                    "a_row r_row b_row k_row decay_end bonus masked0 masked1 masked2 masked3")

        @block.gpsimd
        def _(pool):
            c = Setup(pool, s["const"])
            c.identity(ident)
            c.fill(ones[:, :], 0.0)
            c.fill(ones[0:64, 0:64], 1.0)
            c.fill(ones[64:128, 64:128], 1.0)
            c.fill(mask[:, :, :], 1.0)
            for half in range(2):
                q = slice(64 * half, 64 * half + 64)
                c.keep(mask[q, 0, :], ALU.is_gt, [[1, L]], -1, 0.0)
                c.keep(mask[q, 1, :], ALU.is_ge, [[1, L]], -1, 0.0)
            c.fill(restart[:, :, :], 1.0)
            c.fill(restart[:, :, 0:1], 0.0)
            c.fill(zin[:, :, :, 0:1], 0.0)
            assert c.n == 13

        def stores(sp, m):
            sp.wait_ge(s["act"], ac_.at(m, "gate"))
            sp.dma_start(gate_d[m], gs[:, :]).then_inc(s["st_g"], 16)
            sp.wait_ge(s["dve"], dv_.at(m, "bonus"))
            sp.dma_start(ar_d[:, :, m].rearrange("c p j -> p c j"), ar[:, :, :, :].rearrange("p c a l -> p c (a l)"))\
              .then_inc(s["st_ar"], 16)
            sp.dma_start(bonus_d[m], bon[:, :]).then_inc(s["st_bon"], 16)
            sp.wait_ge(s["dve"], dv_.at(m, "masked3"))
            sp.dma_start(g_d[:, :, 2 * m:2 * m + 2, :].rearrange("c p e j -> p c (e j)"),
                         gm[:, :, :, :].rearrange("p c e j -> p c (e j)")).then_inc(s["st_gm"], 16)
            sp.wait_ge(s["act"], ac_.at(m, "v_copied"))
            sp.dma_start(bk_t_d[:, :, m].rearrange("c p j -> p c j"), bkt[:, :, :]).then_inc(s["st_bkt"], 16)
            sp.dma_start(v_d[:, :, m].rearrange("c p j -> p c j"), vt[:, :, :]).then_inc(s["st_vt"], 16)

        @block.sync
        def _(sp):
            sp.dma_start(rows[0:6 * MB, :], rwkv_mu.rearrange("o i (m p) -> (o i m) p", p=P)).then_inc(s["rows_in"], 16)
            for n, vec in enumerate(vecs):
                sp.dma_start(rows[(6 + n) * MB:(7 + n) * MB, :], vec).then_inc(s["rows_in"], 16)
            for t, d in ((w1, w_lora1), (a1, a_lora1), (g1, g_lora1)):
                sp.dma_start(t[:, :, :], d.rearrange("o (m p) c -> p (o m) c", p=P)).then_inc(s["wl_in"], 16)
            sp.dma_start(w2[:, :], w_lora2[0]).then_inc(s["wl_in"], 16)
            sp.dma_start(a2[:, :], a_lora2[0]).then_inc(s["wl_in"], 16)
            sp.dma_start(g2a[:, :], g_lora2[0, 0:P]).then_inc(s["wl_in"], 16)
            sp.dma_start(g2b[:, :], g_lora2[0, P:160]).then_inc(s["wl_in"], 16)
            sp.wait_ge(s["const"], 13)
            for m in range(MB):
                if m >= 2:
                    sp.wait_ge(s["dve"], p1dve.at(m - 2, "shift"))
                sp.dma_start(zin[:, m % 2, 0, 1:], pv[C0 + m]).then_inc(c_in[m % 2], 16)
            for m in range(MB):
                if m < 2:
                    sp.wait_ge(s["dve"], p1dve.at(MB - 2 + m, "shift"))
                else:
                    sp.wait_ge(s["dve"], dv_.at(m - 2, "shift"))
                for j, b0 in enumerate((R0, K0, V0)):
                    sp.dma_start(zin[:, m % 2, j, 1:], pv[b0 + m]).then_inc(z_in[m % 2], 16)
                if m >= 1:
                    stores(sp, m - 1)
            stores(sp, MB - 1)
            sp.dma_start(decay_d, dec[:, :, :]).then_inc(s["st_end"], 16)
            sp.dma_start(cols_d, col[:, :, :]).then_inc(s["st_end"], 16)
            sp.wait_ge(s["st_end"], 32)
            for n in ("st_g", "st_ar", "st_gm", "st_bkt", "st_vt", "st_bon"):
                sp.wait_ge(s[n], 16 * MB)

        @block.tensor
        def _(pe):
            pe.wait_ge(s["const"], 13)
            pe.wait_ge(s["rows_in"], 16 * (1 + len(PARAMS)))
            pe.transpose(ps[:, 7, 0:NV * MB], rows[:, :], ident[0:NV * MB, 0:NV * MB]).then_inc(s["pe"], 1)
            pe.wait_ge(s["wl_in"], 16 * 7)
            for m in range(MB):
                pe.wait_ge(s["dve"], p1dve.at(m, "shift"))
                st, en = m == 0, m == MB - 1
                pe.matmul(ps[0:64, 0, :], w1[:, m, :], x3[:, m % 2, 0, :], start=st, stop=en)
                pe.matmul(ps[0:64, 1, :], a1[:, m, :], x3[:, m % 2, 1, :], start=st, stop=en)
                pe.matmul(ps[:, 2, :], g1[:, m, 0:P], x3[:, m % 2, 2, :], start=st, stop=en)
                pe.matmul(ps[0:32, 3, :], g1[:, m, P:160], x3[:, m % 2, 2, :], start=st, stop=en)\
                  .then_inc(s["pe"], 1)
            pe.wait_ge(s["act"], AC1)
            for m in range(MB):
                c = slice(m * P, (m + 1) * P)
                if m >= 1:
                    pe.wait_ge(s["act"], ac_.at(m - 1, "v_copied"))
                pe.matmul(ps[:, 0, :], w2[:, c], hw[:, :], start=True, stop=True).then_inc(s["pe"], 1)
                pe.matmul(ps[:, 1, :], a2[:, c], ha[:, :], start=True, stop=True).then_inc(s["pe"], 1)
                pe.matmul(ps[:, 2, :], g2a[:, c], hga[:, :], start=True, stop=False)
                pe.matmul(ps[:, 2, :], g2b[:, c], hgb[:, :], start=False, stop=True).then_inc(s["pe"], 1)
                pe.wait_ge(s["act"], ac_.at(m, "square"))
                pe.matmul(ps[:, 3, :], ones[:, :], sq[:, :], start=True, stop=True).then_inc(s["pe"], 1)
                pe.wait_ge(s["act"], ac_.at(m, "norm"))
                pe.wait_ge(s["dve"], dv_.at(m, "rk_part"))
                pe.matmul(ps[:, 3, :], ones[:, :], tmp[:, :], start=True, stop=True).then_inc(s["pe"], 1)
                pe.wait_ge(s["dve"], dv_.at(m, "bonus"))
                if m >= 1:
                    pe.wait_ge(s["dve"], dv_.at(m - 1, "masked3"))
                for ch in range(NC):
                    for e in range(2):
                        q = slice(64 * e, 64 * e + 64)
                        j = ch % 4
                        mm = pe.matmul(ps[:, 4 + 2 * e + ch // 4, j * P:(j + 1) * P],
                                       bk[q, ch, :, :].rearrange("p a l -> p (a l)"),
                                       ar[q, ch, :, :].rearrange("p a l -> p (a l)"), start=True, stop=True)
                mm.then_inc(s["pe"], 1)
                for ch in range(NC):
                    t = pe.transpose(ps[:, ch // 4, (ch % 4) * P:(ch % 4 + 1) * P],
                                     bk[:, ch, :, :].rearrange("p a l -> p (a l)"), ident[:, :])
                t.then_inc(s["pe"], 1)
                for ch in range(NC):
                    t = pe.transpose(ps[0:64, 2 + ch // 4, (ch % 4) * P:(ch % 4 + 1) * P],
                                     v[:, ch * L:(ch + 1) * L], ident[:, :])
                t.then_inc(s["pe"], 1)

        @block.scalar
        def _(act):
            def par(n, m):
                return col[:, n, m:m + 1]
            act.wait_ge(s["pe"], 1)
            act.copy(col[:, :, :].rearrange("p n m -> p (n m)"), ps[:, 7, 0:NV * MB]).then_inc(s["act"], 1)
            act.wait_ge(s["pe"], p1pe.at(MB - 1, "lora"))
            act.activation(hw[:, :], ps[0:64, 0, :], ACT.Tanh).then_inc(s["act"], 1)
            act.copy(ha[:, :], ps[0:64, 1, :]).then_inc(s["act"], 1)
            act.activation(hga[:, :], ps[:, 2, :], ACT.Sigmoid).then_inc(s["act"], 1)
            act.activation(hgb[:, :], ps[0:32, 3, :], ACT.Sigmoid).then_inc(s["act"], 1)
            act.wait_ge(s["act"], AC0)
            for m in range(MB):
                c = Turn(act, ac_, m)
                act.wait_ge(s["pe"], pe_.at(m, "decay_in"))
                if m >= 1:
                    act.wait_ge(s["dve"], dv_.at(m - 1, "bonus"))
                c.mark("decay_sig", act.activation(sw[:, :], ps[:, 0, :], ACT.Sigmoid, bias=par(6, m)))
                act.wait_ge(s["pe"], pe_.at(m, "rate_in"))
                c.mark("rate", act.activation(av[:, :], ps[:, 1, :], ACT.Sigmoid, bias=par(7, m)))
                act.wait_ge(s["act"], ac_.at(m, "decay_sig"))
                c.mark("log_decay", act.activation(lw[:, :], sw[:, :], ACT.Copy, scale=DECAY))
                act.wait_ge(s["dve"], dv_.at(m, "kk_raw"))
                c.mark("square", act.activation(sq[:, :], kk[:, :], ACT.Square))
                act.wait_ge(s["pe"], pe_.at(m, "gate_in"))
                if m >= 1:
                    act.wait_ge(s["st_g"], 16 * m)
                c.mark("gate", act.copy(gs[:, :], ps[:, 2, :]))
                act.wait_ge(s["pe"], pe_.at(m, "square_sum"))
                c.mark("norm", act.activation(nrm[:, :], ps[:, 3, :], ACT.Sqrt))
                act.wait_ge(s["dve"], dv_.at(m, "cum_prev"))
                c.mark("e_in", act.activation(e_in[:, :], cum[:, :], ACT.Exp))
                c.mark("e_out", act.activation(e_out[:, :], cum[:, :], ACT.Exp, scale=-1.0))
                c.mark("e_prev", act.activation(e_prev[:, :], cumx[:, :], ACT.Exp))
                act.wait_ge(s["pe"], pe_.at(m, "bk_turned"))
                if m >= 1:
                    act.wait_ge(s["st_bkt"], 16 * m)
                    act.wait_ge(s["st_vt"], 16 * m)
                for g in range(2):
                    ins = act.copy(bkt[:, 4 * g:4 * g + 4, :].rearrange("p b j -> p (b j)"), ps[:, g, :])
                c.mark("bk_copied", ins)
                act.wait_ge(s["pe"], pe_.at(m, "v_turned"))
                for g in range(2):
                    ins = act.copy(vt[:, 4 * g:4 * g + 4, :].rearrange("p b j -> p (b j)"), ps[0:64, 2 + g, :])
                c.mark("v_copied", ins)

        @block.vector
        def _(dve):
            def par(n, m):
                return col[:, n, m:m + 1]

            def ch3(t):
                return t.rearrange("p (c l) -> p c l", l=L)

            dve.wait_ge(s["act"], AC0)
            dve.tensor_scalar(ka1[:, :], col[:, 9, :], -1.0, 1.0, ALU.mult, ALU.add).then_inc(s["dve"], 1)
            for m in range(MB):
                c = Turn(dve, p1dve, m)
                u = m % 2
                dve.wait_ge(c_in[u], 16 * (m // 2 + 1))
                c.then("diff", dve.tensor_tensor(dif[:, 0, :], zin[:, u, 0, 0:T], zin[:, u, 0, 1:], ALU.subtract))
                if m >= 2:
                    dve.wait_ge(s["pe"], p1pe.at(m - 2, "lora"))
                for j in range(3):
                    ins = dve.scalar_tensor_tensor(x3[:, u, j, :], dif[:, 0, :], par(3 + j, m), zin[:, u, 0, 1:],
                                                   ALU.mult, ALU.add)
                c.then("shift", ins)
            for m in range(MB):
                c = Turn(dve, dv_, m)
                u = m % 2
                dve.wait_ge(z_in[u], 48 * (m // 2 + 1))
                c.then("diff", dve.tensor_tensor(dif[:, :, :], zin[:, u, :, 0:T], zin[:, u, :, 1:], ALU.subtract))
                if m >= 1:
                    dve.wait_ge(s["pe"], pe_.at(m - 1, "v_turned"))
                for j, dst in enumerate((r, k, v)):
                    ins = dve.scalar_tensor_tensor(dst[:, :], dif[:, j, :], par(j, m), zin[:, u, j, 1:],
                                                   ALU.mult, ALU.add)
                c.then("shift", ins)
                c.mark("kk_raw", dve.tensor_scalar(kk[:, :], k[:, :], par(8, m), None, ALU.mult))
                dve.wait_ge(s["act"], ac_.at(m, "log_decay"))
                c.then("cum", dve.tensor_tensor_scan(cum[:, :], restart[:, :, :].rearrange("p c l -> p (c l)"),
                                                     lw[:, :], 0.0, ALU.mult, ALU.add))
                c.mark("cum_prev", dve.tensor_tensor(cumx[:, :], cum[:, :], lw[:, :], ALU.subtract))
                c.then("k_part", dve.tensor_scalar(k2[:, :], av[:, :], par(9, m), ka1[:, m:m + 1], ALU.mult, ALU.add))
                c.then("k_new", dve.tensor_tensor(k2[:, :], k2[:, :], k[:, :], ALU.mult))
                dve.wait_ge(s["act"], ac_.at(m, "norm"))
                c.then("norm_max", dve.tensor_scalar(nrm[:, :], nrm[:, :], 1e-12, None, ALU.max))
                c.then("norm_inv", dve.reciprocal(nrm[:, :], nrm[:, :]))
                c.then("kk", dve.tensor_tensor(kk[:, :], kk[:, :], nrm[:, :], ALU.mult))
                c.mark("kk_a", dve.tensor_tensor(dif[:, 0, :], kk[:, :], av[:, :], ALU.mult))
                c.then("rk_part", dve.scalar_tensor_tensor(tmp[:, :], r[:, :], par(10, m), k2[:, :],
                                                           ALU.mult, ALU.mult))
                dve.wait_ge(s["act"], ac_.at(m, "e_prev"))
                if m >= 1:
                    dve.wait_ge(s["st_ar"], 16 * m)
                    dve.wait_ge(s["st_bon"], 16 * m)
                c.mark("a_row", dve.scalar_tensor_tensor(ar[:, :, 0, :], ch3(kk[:, :]), -1.0, ch3(e_prev[:, :]),
                                                         ALU.mult, ALU.mult))
                c.mark("r_row", dve.tensor_tensor(ar[:, :, 1, :], ch3(r[:, :]), ch3(e_in[:, :]), ALU.mult))
                c.mark("b_row", dve.tensor_tensor(bk[:, :, 0, :], ch3(dif[:, 0, :]), ch3(e_out[:, :]), ALU.mult))
                c.mark("k_row", dve.tensor_tensor(bk[:, :, 1, :], ch3(k2[:, :]), ch3(e_out[:, :]), ALU.mult))
                c.mark("decay_end", dve.tensor_copy(dec[:, m, :], ch3(e_in[:, :])[:, :, L - 1]))
                dve.wait_ge(s["pe"], pe_.at(m, "bonus_sum"))
                c.mark("bonus", dve.tensor_tensor(bon[:, :], ps[:, 3, :], v[:, :], ALU.mult))
                dve.wait_ge(s["pe"], pe_.at(m, "chunks"))
                if m >= 1:
                    dve.wait_ge(s["st_gm"], 16 * m)
                for g in range(4):
                    c.mark(f"masked{g}", dve.tensor_tensor(
                        gm[:, 4 * (g % 2):4 * (g % 2) + 4, g // 2, :],
                        ps[:, 4 + g, :].rearrange("p (a j) -> p a j", j=2 * L),
                        mask[:, :, :].rearrange("p a l -> p (a l)").unsqueeze(1).broadcast_to([P, 4, 2 * L]),
                        ALU.mult))


class Inverse:

    def __init__(self, sb, sem, g_d, wt_d):
        self.g_d, self.wt_d = g_d, wt_d
        self.at = sb("at", [P, L, L])
        self.wt = sb("wt", [P, L, L])
        self.prod = sb("prod", [P, L * L])
        self.a_in, self.row, self.stored = sem("a_in"), sem("row"), sem("wt_stored")

    def load(self, sp):
        for c in range(NC):
            sp.dma_start(self.at[H * c:H * c + H, :, :], self.g_d[c, 0:L, :, 0:L].rearrange("s h t -> h s t"))\
              .then_inc(self.a_in, 16)

    def store(self, sp):
        sp.wait_ge(self.row, 2 * L)
        for c in range(NC):
            sp.dma_start(self.wt_d[c].rearrange("j h t -> h j t"), self.wt[H * c:H * c + H, :, :])\
              .then_inc(self.stored, 16)

    def finish(self, sp):
        sp.wait_ge(self.stored, 16 * NC)

    def vector(self, dve):
        at, wt, row = self.at, self.wt, self.row
        dve.memset(wt[:, :, :], 0.0).then_inc(row, 1)
        dve.wait_ge(row, 1)
        dve.memset(wt[:, :, :].rearrange("p j t -> p (j t)")[:, 0:L * L:L + 1], 1.0).then_inc(row, 1)
        dve.wait_ge(row, 2)
        dve.wait_ge(self.a_in, 16 * NC)
        for t in range(1, L):
            tile = self.prod[:, 0:t * t].rearrange("p (j s) -> p j s", s=t)
            dve.tensor_tensor(tile, wt[:, 0:t, 0:t], at[:, 0:t, t].unsqueeze(1).broadcast_to([P, t, t]), ALU.mult)\
               .then_inc(row, 1)
            dve.wait_ge(row, 2 * t + 1)
            dve.tensor_reduce(wt[:, 0:t, t], tile, AX, ALU.add).then_inc(row, 1)
            dve.wait_ge(row, 2 * t + 2)


def rwkv_scan(nc, ar_d, bk_t_d, g_d, v_d, decay_d, wt_d, y_d):
    with ExitStack() as ctx:
        def sb(name, shape, dt=F32):
            return ctx.enter_context(nc.sbuf_tensor("s_" + name, shape, dt))

        sem = semaphores(nc, ctx, "s_")
        ar = [sb(f"ar{u}", [P, MB, 2 * L]) for u in range(2)]
        bkt = [sb(f"bkt{u}", [P, MB, P]) for u in range(2)]
        g = [sb(f"g{u}", [P, H, 2 * L]) for u in range(2)]
        wt = [sb(f"wt{u}", [L, H, L]) for u in range(2)]
        uv = [sb(f"uv{u}", [P, H, HD]) for u in range(2)]
        xs = sb("xs", [L, H, HD])
        ys = [sb(f"ys{u}", [L, H * HD]) for u in range(2)]
        state = sb("state", [P, MB, P])
        hsum = sb("hsum", [P, MB, HD])
        dec = sb("dec", [P, MB, NC])
        ps = ctx.enter_context(nc.psum_tensor("s_ps", [P, 8, T], F32))
        loaded = [sem(f"loaded{u}") for u in range(2)]
        dec_in, zeroed, seq = sem("dec_in"), sem("zeroed"), sem("seq")
        y_out = [sem(f"y_out{u}") for u in range(2)]
        pe_ = Steps(sem("pe"), 0, "x0 x1 u0 u1 state0 state1 y0 y1")
        dv_ = Steps(sem("dve"), 1, "x0 u0 add0 add1 decay0 decay1")
        ac_ = Steps(sem("act"), 1, "x1 u1 y0 y1")
        block = ctx.enter_context(nc.Block())
        flat = ps[:, :, :].rearrange("p b t -> p (b t)")

        def bank_pair(n):
            return flat[:, 2 * T * n:2 * T * (n + 1)]

        X, U, Y, S = (bank_pair(n) for n in range(4))

        @block.sync
        def _(sp):
            sp.dma_start(dec[:, :, :], decay_d).then_inc(dec_in, 16)

            def load(turn, u):
                def at(d):
                    return d[turn] if isinstance(turn, int) else \
                        d[bass.ds(turn, 1)].rearrange("o p a b -> (o p) a b")
                sp.dma_start(ar[u][:, :, :], at(ar_d)).then_inc(loaded[u], 16)
                sp.dma_start(g[u][:, :, :], at(g_d)).then_inc(loaded[u], 16)
                sp.dma_start(uv[u][L:P, :, :].rearrange("s (m e) j -> s m (e j)", e=2), at(v_d)).then_inc(loaded[u], 16)
                sp.dma_start(wt[u][:, :, :], at(wt_d)).then_inc(loaded[u], 16)
                sp.dma_start(bkt[u][:, :, :], at(bk_t_d)).then_inc(loaded[u], 16)
            for u in range(2):
                load(u, u)
            with sp.Fori(0, NC // 2 - 1) as i:
                for u in range(2):
                    sp.wait_ge(pe_.sem, pe_.at(i * 2 + u, "y1"))
                    load(i * 2 + (u + 2), u)

        @block.gpsimd
        def _(pool):
            for u in range(2):
                pool.memset(uv[u][0:L, :, :], 0.0).then_inc(zeroed, 1)
            with pool.Fori(0, NC // 2 - 1) as i:
                for u in range(2):
                    pool.wait_ge(pe_.sem, pe_.at(i * 2 + u, "y1"))
                    pool.sem_inc(seq, 1)
                    pool.memset(uv[u][0:L, :, :], 0.0).then_inc(zeroed, 1)

        @block.tensor
        def _(pe):
            with pe.Fori(0, NC // 2) as i:
                for u in range(2):
                    n = i * 2 + u
                    pe.wait_ge(loaded[u], i * 80 + 80)
                    pe.wait_ge(zeroed, n + 1)
                    pe.wait_ge(dv_.sem, n * 6 + 1)
                    for m in range(MB):
                        pe.matmul(X[0:L, m * P:(m + 1) * P], ar[u][:, m, 0:L], state[:, m, :],
                                  start=True, stop=False, skip_group_check=True)
                        for e in range(2):
                            h = 2 * m + e
                            mm = pe.matmul(X[0:L, h * HD:(h + 1) * HD], g[u][:, h, 0:L], uv[u][:, h, :],
                                           start=False, stop=True, skip_group_check=True)
                        if m % 4 == 3:
                            mm.then_inc(pe_.sem, 1)
                    for half in range(2):
                        if half == 0:
                            pe.wait_ge(dv_.sem, dv_.at(n, "x0"))
                        else:
                            pe.wait_ge(ac_.sem, ac_.at(n, "x1"))
                        pe.sem_inc(seq, 1)
                        for h in range(8 * half, 8 * half + 8):
                            mm = pe.matmul(U[0:L, h * HD:(h + 1) * HD], wt[u][:, h, :], xs[:, h, :],
                                           start=True, stop=True)
                        mm.then_inc(pe_.sem, 1)
                    for half in range(2):
                        if half == 0:
                            pe.wait_ge(dv_.sem, dv_.at(n, "u0"))
                        else:
                            pe.wait_ge(ac_.sem, ac_.at(n, "u1"))
                        for m in range(4 * half, 4 * half + 4):
                            mm = pe.matmul(S[:, m * P:(m + 1) * P], bkt[u][:, m, :],
                                           uv[u][:, 2 * m:2 * m + 2, :].rearrange("p e j -> p (e j)"),
                                           start=True, stop=True)
                        mm.then_inc(pe_.sem, 1)
                    pe.wait_ge(ac_.sem, n * 4 + 1)
                    for m in range(MB):
                        pe.matmul(Y[0:L, m * P:(m + 1) * P], ar[u][:, m, L:2 * L], state[:, m, :],
                                  start=True, stop=False, skip_group_check=True)
                        for e in range(2):
                            h = 2 * m + e
                            mm = pe.matmul(Y[0:L, h * HD:(h + 1) * HD], g[u][:, h, L:2 * L], uv[u][:, h, :],
                                           start=False, stop=True, skip_group_check=True)
                        if m % 4 == 3:
                            mm.then_inc(pe_.sem, 1)

        @block.scalar
        def _(act):
            act.sem_inc(ac_.sem, 1)
            for u in range(2):
                act.sem_inc(y_out[u], 16)
            hw = 8 * HD
            with act.Fori(0, NC // 2) as i:
                for u in range(2):
                    c = Turn(act, ac_, i * 2 + u)
                    act.wait_ge(pe_.sem, pe_.at(c.turn, "x1"))
                    c.mark("x1", act.copy(xs[:, 8:16, :].rearrange("p h j -> p (h j)"), X[0:L, hw:2 * hw]))
                    act.wait_ge(pe_.sem, pe_.at(c.turn, "u1"))
                    c.mark("u1", act.copy(uv[u][0:L, 8:16, :].rearrange("p h j -> p (h j)"), U[0:L, hw:2 * hw]))
                    act.wait_ge(y_out[u], i * 16 + 16)
                    for half in range(2):
                        act.wait_ge(pe_.sem, pe_.at(c.turn, f"y{half}"))
                        c.mark(f"y{half}", act.copy(ys[u][:, half * hw:(half + 1) * hw],
                                                    Y[0:L, half * hw:(half + 1) * hw]))
                    act.wait_ge(ac_.sem, ac_.at(c.turn, "y1"))
                    act.dma_start(y_d.rearrange("(c l) j -> c l j", l=L)[bass.ds(i * 2 + u, 1)]
                                  .rearrange("o l j -> (o l) j"), ys[u][:, :]).then_inc(y_out[u], 16)
            for u in range(2):
                act.wait_ge(y_out[u], 16 * (NC // 2) + 16)

        @block.vector
        def _(dve):
            dve.memset(state[:, :, :], 0.0).then_inc(dv_.sem, 1)
            dve.wait_ge(dec_in, 16)
            hw = 8 * HD
            with dve.Fori(0, NC // 2) as i:
                for u in range(2):
                    n = i * 2 + u
                    c = Turn(dve, dv_, n)
                    dve.wait_ge(pe_.sem, pe_.at(n, "x0"))
                    c.mark("x0", dve.tensor_copy(xs[:, 0:8, :].rearrange("p h j -> p (h j)"), X[0:L, 0:hw]))
                    dve.wait_ge(pe_.sem, pe_.at(n, "u0"))
                    c.mark("u0", dve.tensor_copy(uv[u][0:L, 0:8, :].rearrange("p h j -> p (h j)"), U[0:L, 0:hw]))
                    dve.wait_ge(pe_.sem, pe_.at(n, "state1"))
                    for e in range(2):
                        q, k = slice(64 * e, 64 * e + 64), slice(HD * e, HD * e + HD)
                        c.mark(f"add{e}", dve.tensor_tensor(
                            hsum[q, :, :], S.rearrange("p (m j) -> p m j", j=P)[q, :, k], state[q, :, k], ALU.add))
                    dve.wait_ge(pe_.sem, pe_.at(n, "y1"))
                    dve.wait_ge(dv_.sem, dv_.at(n, "add1"))
                    for e in range(2):
                        q, k = slice(64 * e, 64 * e + 64), slice(HD * e, HD * e + HD)
                        c.mark(f"decay{e}", dve.tensor_tensor(
                            state[q, :, k], hsum[q, :, :], dec[q, :, bass.ds(n, 1)].broadcast_to([64, MB, HD]),
                            ALU.mult))


NPAIR = MB
EXP_LN_SET = 6


def attention_and_inverse(nc, proj_t, at_d, g_d, wt_d):
    pv = proj_t.rearrange("(b p) t -> b p t", p=P)
    width = [T - P * j for j in range(NB)]
    at0 = [sum(width[:j]) for j in range(NB)]
    TOTAL = sum(width)
    with ExitStack() as ctx:
        def sb(name, shape, dt=F32):
            return ctx.enter_context(nc.sbuf_tensor("d_" + name, shape, dt))

        sem = semaphores(nc, ctx, "d_")
        ident = sb("ident", [P, P])
        tri = sb("tri", [P, P])
        neg = sb("neg", [P, P])
        qkv = [sb(f"qkv{b}", [P, 3, T]) for b in range(2)]
        qs = [sb(f"qs{b}", [P, T]) for b in range(2)]
        vt = [sb(f"vt{b}", [P, NB, P]) for b in range(2)]
        na = [sb(f"na{e}", [P, TOTAL]) for e in range(2)]
        sp_ = [sb(f"sp{e}", [P, NB, T]) for e in range(2)]
        w = [sb(f"w{e}", [P, NB, T]) for e in range(2)]
        oc = [sb(f"oc{b}", [P, T]) for b in range(2)]
        ps = ctx.enter_context(nc.psum_tensor("d_ps", [P, 8, T], F32))
        re = [sb(f"re{e}", [P, TOTAL]) for e in range(2)]
        inverse = Inverse(sb, sem, g_d, wt_d)
        const, scaled, v_turned, v_copied = sem("const"), sem("scaled"), sem("v_turned"), sem("v_copied")
        qkv_in = [sem(f"qkv_in{b}") for b in range(2)]
        out_stored = [sem(f"out_stored{b}") for b in range(2)]
        (z_done, abs_done, exp_done, ln_done, sp_done, sp_masked, sum_done, w_done, w_masked, out_done, copied) = (
            [sem(f"{n}{e}") for e in range(2)] for n in (
                "z_done", "abs_done", "exp_done", "ln_done", "sp_done", "sp_masked", "sum_done", "w_done",
                "w_masked", "out_done", "copied"))
        pool_turn = sem("pool_turn")
        block = ctx.enter_context(nc.Block())

        def dram(p, first):
            if isinstance(p, int):
                return pv[first + p]
            return pv[bass.ds(p + first, 1)].rearrange("o p t -> (o p) t")

        def looped(eng, before, body):
            before()
            with eng.Fori(0, NPAIR // 2 - 1) as i:
                for b in range(2):
                    body(i * 2 + b, b, True)
            for b in range(2):
                body(NPAIR - 2 + b, b, b == 0)

        @block.sync
        def _(sp):
            def load(p, b):
                for n in range(3):
                    sp.dma_start(qkv[b][:, n, :], dram(p, n * MB)).then_inc(qkv_in[b], 16)

            def store(p, b):
                for e in range(2):
                    sp.wait_ge(copied[e], p + 1)
                d = at_d[p] if isinstance(p, int) else at_d[bass.ds(p, 1)].rearrange("o p t -> (o p) t")
                sp.dma_start(d, oc[b][:, :]).then_inc(out_stored[b], 16)
            for b in range(2):
                sp.sem_inc(out_stored[b], 16)
                load(b, b)
            inverse.load(sp)
            with sp.Fori(0, NPAIR // 2 - 1) as i:
                for b in range(2):
                    sp.wait_ge(z_done[1], i * 2 + (b + 1))
                    load(i * 2 + (b + 2), b)
                for b in range(2):
                    store(i * 2 + b, b)
            inverse.store(sp)
            for b in range(2):
                store(NPAIR - 2 + b, b)
            for b in range(2):
                sp.wait_ge(out_stored[b], 16 * (NPAIR // 2) + 16)
            inverse.finish(sp)

        @block.gpsimd
        def _(pool):
            c = Setup(pool, const)
            c.identity(ident)
            c.fill(neg[:, :], -1.0)
            c.fill(tri[:, :], -1.0)
            c.keep(tri[:, :], ALU.is_ge, [[-1, P]], 1, 0.0)
            assert c.n == 5

            def causal(tile, done):
                pool.affine_select(out=tile[:, :, 0:P], in_=tile[:, :, 0:P], compare_op=ALU.is_gt, fill=0.0,
                                   base=0, pattern=[[0, NB], [1, P]], channel_multiplier=-1).then_inc(done, 1)

            def first(p, e):
                pool.wait_ge(sum_done[e], p + 1)
                pool.wait_ge(ln_done[e], p + 1)
                pool.sem_inc(pool_turn, 1)
                for j in range(NB):
                    a = slice(at0[j], at0[j] + width[j])
                    ins = pool.tensor_tensor(sp_[e][:, j, 0:width[j]], re[e][:, a], na[e][:, a], ALU.add)
                ins.then_inc(sp_done[e], 1)
                pool.wait_ge(sp_done[e], p + 2)
                pool.sem_inc(pool_turn, 1)
                causal(sp_[e], sp_masked[e])

            def second(p, e):
                pool.wait_ge(w_done[e], p + 1)
                pool.sem_inc(pool_turn, 1)
                causal(w[e], w_masked[e])
            def before():
                for e in range(2):
                    pool.sem_inc(sp_done[e], 1)
                for e in range(2):
                    first(0, e)

            def body(p, b, more):
                for e in range(2):
                    second(p, e)
                if more:
                    for e in range(2):
                        first(p + 1, e)
            looped(pool, before, body)

        @block.tensor
        def _(pe):
            def scores(p, b, e):
                pe.wait_ge(qkv_in[b], (p - b) * 24 + 48)
                pe.wait_ge(scaled, p + 1)
                if e == 0:
                    pe.wait_ge(v_copied, p)
                    pe.wait_ge(copied[0], p)
                    for j in range(NB):
                        o = ps[:, 3, P * (j + 1):P * (j + 2)] if j < 3 else ps[:, 2, 2 * P:3 * P]
                        t = pe.transpose(o, qkv[b][:, 2, j * P:(j + 1) * P], ident[:, :])
                    t.then_inc(v_turned, 1)
                pe.wait_ge(copied[e], p)
                r = slice(64 * e, 64 * e + 64)
                for j in range(NB):
                    mm = pe.matmul(ps[:, 4 * e + j, 0:width[j]], qkv[b][r, 1, j * P:(j + 1) * P],
                                   qs[b][r, j * P:T], start=True, stop=False, skip_group_check=True)
                mm.then_inc(z_done[e], 1)

            def sums(p, e):
                pe.wait_ge(sp_masked[e], p + 1)
                for j in range(NB):
                    for i in range(j, NB):
                        mm = pe.matmul(ps[:, 4 * e + j, (i - j) * P:width[j]], (tri if i == j else neg)[:, :],
                                       sp_[e][:, i, 0:width[i]], start=False, stop=(i == NB - 1),
                                       skip_group_check=True)
                mm.then_inc(sum_done[e], 1)

            def values(p, b, e):
                pe.wait_ge(v_copied, p + 1)
                pe.wait_ge(w_masked[e], p + 1)
                for j in range(NB):
                    mm = pe.matmul(ps[:, 4 * e, j * P:T], vt[b][:, j, :], w[e][:, j, 0:width[j]],
                                   start=(j == 0), stop=(j == NB - 1), skip_group_check=True)
                mm.then_inc(out_done[e], 1)

            def before():
                for e in range(2):
                    pe.sem_inc(sum_done[e], 1)
                    pe.sem_inc(out_done[e], 1)
                pe.wait_ge(const, 5)
                scores(0, 0, 0)
                scores(0, 0, 1)

            def body(p, b, more):
                sums(p, 0)
                sums(p, 1)
                for e in range(2):
                    values(p, b, e)
                    if more:
                        scores(p + 1, 1 - b, e)
            looped(pe, before, body)

        @block.scalar
        def _(act):
            def scale(p, b):
                act.wait_ge(qkv_in[b], (p - b) * 24 + 48)
                act.activation(qs[b][:, :], qkv[b][:, 0, :], ACT.Copy, scale=HD ** -0.5).then_inc(scaled, 1)

            def first(p, e, b):
                if e == 0:
                    act.wait_ge(v_turned, p + 1)
                    act.wait_ge(z_done[0], p + 1)
                    act.copy(vt[b][:, 0:3, :].rearrange("p j d -> p (j d)"), ps[:, 3, P:T])
                    act.copy(vt[b][:, 3, :], ps[:, 2, 2 * P:3 * P]).then_inc(v_copied, 1)
                act.wait_ge(z_done[e], p + 1)
                act.wait_ge(sp_done[e], p + 1)
                for j in range(NB):
                    a = slice(at0[j], at0[j] + width[j])
                    act.activation(re[e][:, a], ps[:, 4 * e + j, 0:width[j]], ACT.Relu)
                    ins = act.activation(na[e][:, a], ps[:, 4 * e + j, 0:width[j]], ACT.Abs)
                ins.then_inc(abs_done[e], 1)
                act.wait_ge(abs_done[e], p + 1)
                act.activation(na[e][:, :], na[e][:, :], ACT.Exp, scale=-1.0).then_inc(exp_done[e], 1)
                act.wait_ge(exp_done[e], p + 1)
                act.activation(na[e][:, :], na[e][:, :], ACT.Ln, bias=1.0).then_inc(ln_done[e], 1)

            def second(p, e):
                act.wait_ge(out_done[e], p + 1)
                act.wait_ge(sum_done[e], p + 2)
                for j in range(NB):
                    ins = act.activation(w[e][:, j, 0:width[j]], ps[:, 4 * e + j, 0:width[j]], ACT.Exp)
                ins.then_inc(w_done[e], 1)

            def third(p, b, e):
                act.wait_ge(out_stored[b], (p - b) * 8 + 16)
                act.wait_ge(out_done[e], p + 2)
                r = slice(64 * e, 64 * e + 64)
                act.copy(oc[b][r, :], ps[r, 4 * e, :]).then_inc(copied[e], 1)

            def before():
                act.add_instruction(mybir.InstLoadActFuncSet(
                    act_func_set_id=EXP_LN_SET, name=nc.get_next_instruction_name(),
                    engine=mybir.EngineType.Activation, ins=[], outs=[]))
                scale(0, 0)
                first(0, 0, 0)
                first(0, 1, 0)

            def body(p, b, more):
                if more:
                    scale(p + 1, 1 - b)
                second(p, 0)
                second(p, 1)
                for e in range(2):
                    third(p, b, e)
                    if more:
                        first(p + 1, e, 1 - b)
            looped(act, before, body)

        @block.vector
        def _(dve):
            inverse.vector(dve)


GN_EPS = 64e-5
LN_EPS = 1e-5
ALPHA = 2 ** 0.25
GATE_A, GATE_B = 7 * MB, 7 * MB + KT


def rwkv_finish(nc, y_d, cols_d, bonus_d, gate_d, yb):
    with ExitStack() as ctx:
        def sb(name, shape, dt=F32):
            return ctx.enter_context(nc.sbuf_tensor("e_" + name, shape, dt))

        sem = semaphores(nc, ctx, "e_")
        ident = sb("ident", [P, P])
        y = sb("y", [P, NB, W])
        sq = sb("sq", [P, NB, W])
        bonus = sb("bonus", [P, MB, T])
        gate = sb("gate", [P, MB, T])
        col = sb("col", [P, 13, MB])
        mean = sb("mean", [P, NB, H])
        var = sb("var", [P, NB, H])
        ps = ctx.enter_context(nc.psum_tensor("e_ps", [P, 8, T], F32))
        const, y_in, rest_in = sem("const"), [sem(f"y_in{n}") for n in range(NB)], sem("rest_in")
        dv_ = Steps(sem("dve"), 0, "sum mean centre sumsq var inv norm")
        ac_ = Steps(sem("act"), 0, "square root")
        turned, scaled, out = sem("turned"), sem("scaled"), sem("out")
        block = ctx.enter_context(nc.Block())

        @block.gpsimd
        def _(pool):
            Setup(pool, const).identity(ident)

        @block.sync
        def _(sp):
            yv = y_d.rearrange("(n p) j -> n p j", p=P)
            for n in range(NB):
                sp.dma_start(y[:, n, :], yv[n]).then_inc(y_in[n], 16)
            sp.dma_start(col[:, :, :], cols_d).then_inc(rest_in, 16)
            sp.dma_start(bonus[:, :, :], bonus_d.rearrange("m p t -> p m t")).then_inc(rest_in, 16)
            sp.dma_start(gate[:, :, :], gate_d.rearrange("m p t -> p m t")).then_inc(rest_in, 16)

        @block.vector
        def _(dve):
            for n in range(NB):
                c = Turn(dve, dv_, n)
                yn = y[:, n, :].rearrange("p (h j) -> p h j", j=HD)
                sn = sq[:, n, :].rearrange("p (h j) -> p h j", j=HD)
                dve.wait_ge(y_in[n], 16)
                c.then("sum", dve.tensor_reduce(mean[:, n, :], yn, AX, ALU.add))
                c.then("mean", dve.tensor_scalar(mean[:, n, :], mean[:, n, :], 1.0 / HD, None, ALU.mult))
                c.mark("centre", dve.tensor_tensor(yn, yn, mean[:, n, :].unsqueeze(2).broadcast_to([P, H, HD]),
                                                   ALU.subtract))
                dve.wait_ge(ac_.sem, ac_.at(n, "square"))
                c.then("sumsq", dve.tensor_reduce(var[:, n, :], sn, AX, ALU.add))
                c.mark("var", dve.tensor_scalar(var[:, n, :], var[:, n, :], 1.0 / HD, GN_EPS, ALU.mult, ALU.add))
                dve.wait_ge(ac_.sem, ac_.at(n, "root"))
                c.then("inv", dve.reciprocal(var[:, n, :], var[:, n, :]))
                c.mark("norm", dve.tensor_tensor(yn, yn, var[:, n, :].unsqueeze(2).broadcast_to([P, H, HD]),
                                                 ALU.mult))
            for m in range(MB):
                dve.wait_ge(scaled, m + 1)
                dve.tensor_tensor(yb[:, m, :], yb[:, m, :], bonus[:, m, :], ALU.add).then_inc(out, 1)
                dve.wait_ge(out, 2 * m + 1)
                dve.tensor_tensor(yb[:, m, :], yb[:, m, :], gate[:, m, :], ALU.mult).then_inc(out, 1)

        @block.scalar
        def _(act):
            for n in range(NB):
                c = Turn(act, ac_, n)
                act.wait_ge(dv_.sem, dv_.at(n, "centre"))
                c.mark("square", act.activation(sq[:, n, :], y[:, n, :], ACT.Square))
                act.wait_ge(dv_.sem, dv_.at(n, "var"))
                c.mark("root", act.activation(var[:, n, :], var[:, n, :], ACT.Sqrt))
            act.wait_ge(rest_in, 48)
            for m in range(MB):
                act.wait_ge(turned, m + 1)
                act.activation(yb[:, m, :], ps[:, m, :], ACT.Identity, bias=col[:, 12, m:m + 1],
                               scale=col[:, 11, m:m + 1]).then_inc(scaled, 1)

        @block.tensor
        def _(pe):
            pe.wait_ge(const, 2)
            pe.wait_ge(dv_.sem, dv_.at(NB - 1, "norm"))
            for m in range(MB):
                for n in range(NB):
                    t = pe.transpose(ps[:, m, n * P:(n + 1) * P], y[:, n, m * P:(m + 1) * P], ident[:, :])
                t.then_inc(turned, 1)


def mix(nc, proj_t, at_d, yb, w_up_a, w_up_b, mixed):
    GB, GW, G = 4, 512, D // 512
    with ExitStack() as ctx:
        def sb(name, shape, dt=F32):
            return ctx.enter_context(nc.sbuf_tensor("m_" + name, shape, dt))

        sem = semaphores(nc, ctx, "m_")
        at = sb("at", [P, MB, T])
        w = [[sb(f"w{u}{s}", [P, MB, GW]) for s in range(2)] for u in range(2)]
        gt = [sb(f"gt{u}", [P, 2, GB, T]) for u in range(2)]
        other = [sb(f"other{u}", [P, T]) for u in range(2)]
        ps = ctx.enter_context(nc.psum_tensor("m_ps", [P, 8, T], F32))
        at_in = sem("at_in")
        w_in = [[sem(f"w_in{u}{s}") for s in range(2)] for u in range(2)]
        gt_in = [sem(f"gt_in{u}") for u in range(2)]
        made, opened, gated = sem("made"), sem("opened"), sem("gated")
        block = ctx.enter_context(nc.Block())
        wv = [z.rearrange("o (k p) (g c) -> g p (o k) c", p=P, c=GW) for z in (w_up_a, w_up_b)]
        gv = [proj_t[P * b:P * (b + KT)].rearrange("(g b p) t -> g p b t", p=P, b=GB) for b in (GATE_A, GATE_B)]

        @block.sync
        def _(sp):
            sp.dma_start(at[:, :, :], at_d.rearrange("m p t -> p m t")).then_inc(at_in, 16)
            for g in range(G):
                u = g % 2
                if g >= 2:
                    sp.wait_ge(made, 2 * GB * (g - 1))
                for s in range(2):
                    sp.dma_start(w[u][s][:, :, :], wv[s][g]).then_inc(w_in[u][s], 16)
                if g >= 2:
                    sp.wait_ge(gated, 3 * GB * (g - 1))
                for s in range(2):
                    sp.dma_start(gt[u][:, s, :, :], gv[s][g]).then_inc(gt_in[u], 16)

        @block.tensor
        def _(pe):
            pe.wait_ge(at_in, 16)
            for g in range(G):
                for b in range(GB):
                    j = GB * g + b
                    for s, rhs in enumerate((at, yb)):
                        pe.wait_ge(w_in[g % 2][s], 16 * (g // 2 + 1))
                        if j >= 4:
                            pe.wait_ge(gated, 3 * (j - 3))
                        for k in range(MB):
                            mm = pe.matmul(ps[:, 2 * (j % 4) + s, :], w[g % 2][s][:, k, b * P:(b + 1) * P],
                                           rhs[:, k, :], start=(k == 0), stop=(k == MB - 1))
                        mm.then_inc(made, 1)

        @block.scalar
        def _(act):
            for g in range(G):
                act.wait_ge(gt_in[g % 2], 32 * (g // 2 + 1))
                act.activation(gt[g % 2][:, :, :, :], gt[g % 2][:, :, :, :], ACT.Sigmoid).then_inc(opened, 1)

        @block.vector
        def _(dve):
            for j in range(KT):
                g, b = divmod(j, GB)
                dve.wait_ge(opened, g + 1)
                dve.wait_ge(made, 2 * j + 1)
                dve.tensor_tensor(mixed[:, j, :], ps[:, 2 * (j % 4), :], gt[g % 2][:, 0, b, :], ALU.mult)\
                   .then_inc(gated, 1)
                dve.wait_ge(made, 2 * j + 2)
                dve.tensor_tensor(other[j % 2][:, :], ps[:, 2 * (j % 4) + 1, :], gt[g % 2][:, 1, b, :], ALU.mult)\
                   .then_inc(gated, 1)
                dve.wait_ge(gated, 3 * j + 2)
                dve.tensor_tensor(mixed[:, j, :], mixed[:, j, :], other[j % 2][:, :], ALU.add).then_inc(gated, 1)


class Norm:

    def __init__(self, nc, ctx, prefix, sem):
        self.stats = [ctx.enter_context(nc.sbuf_tensor(f"{prefix}_stats{u}", [P, 4, 6], F32)) for u in range(2)]
        self.mv = [ctx.enter_context(nc.sbuf_tensor(f"{prefix}_mv{u}", [P, 2], F32)) for u in range(2)]
        self.steps = Steps(sem("norm"), 0, "stats moments eps inv centre gain shift")
        self.root = sem("root")

    def vector(self, dve, n, x, gain, shift):
        st, mv = self.stats[n % 2], self.mv[n % 2]
        c = Turn(dve, self.steps, n)
        for j in range(4):
            ins = dve.bn_stats(st[:, j, :], x[:, 512 * j:512 * (j + 1)])
        c.then("stats", ins)
        c.then("moments", dve.bn_aggr(mv[:, :], st[:, :, :].rearrange("p a b -> p (a b)")))
        c.mark("eps", dve.tensor_scalar(mv[:, 1:2], mv[:, 1:2], LN_EPS, None, ALU.add))
        dve.wait_ge(self.root, n + 1)
        c.then("inv", dve.reciprocal(mv[:, 1:2], mv[:, 1:2]))
        c.then("centre", dve.tensor_scalar(x, x, mv[:, 0:1], mv[:, 1:2], ALU.subtract, ALU.mult))
        c.then("gain", dve.tensor_tensor(x, x, gain, ALU.mult))
        c.mark("shift", dve.tensor_tensor(x, x, shift, ALU.add))

    def scalar(self, act, n):
        mv = self.mv[n % 2]
        act.wait_ge(self.steps.sem, self.steps.at(n, "eps"))
        act.activation(mv[:, 1:2], mv[:, 1:2], ACT.Sqrt).then_inc(self.root, 1)


def out_project(nc, mixed, w_o, x, ln_w, ln_b, x1_d, x1t):
    GW, G = 512, D // 512
    with ExitStack() as ctx:
        def sb(name, shape, dt=F32):
            return ctx.enter_context(nc.sbuf_tensor("o_" + name, shape, dt))

        sem = semaphores(nc, ctx, "o_")
        ident = sb("ident", [P, P])
        w = [sb(f"w{u}", [P, KT, GW]) for u in range(2)]
        res = sb("res", [P, NB, D])
        gain, shift = sb("gain", [P, D]), sb("shift", [P, D])
        norm = Norm(nc, ctx, "o", sem)
        ps = ctx.enter_context(nc.psum_tensor("o_ps", [P, 8, T], F32))
        const, x_in, ln_in = sem("const"), sem("x_in"), sem("ln_in")
        w_in = [sem(f"w_in{u}") for u in range(2)]
        made, added, turned, kept, stored = sem("made"), sem("added"), sem("turned"), sem("kept"), sem("stored")
        block = ctx.enter_context(nc.Block())
        wv = w_o.rearrange("o (k p) (g c) -> g p (o k) c", p=P, c=GW)

        @block.gpsimd
        def _(pool):
            Setup(pool, const).identity(ident)

        @block.sync
        def _(sp):
            for g in range(G):
                if g >= 2:
                    sp.wait_ge(made, NB * (g - 1))
                sp.dma_start(w[g % 2][:, :, :], wv[g]).then_inc(w_in[g % 2], 16)
                if g == 0:
                    sp.dma_start(res[:, :, :], x.rearrange("o (n p) d -> p (o n) d", p=P)).then_inc(x_in, 16)
                    sp.dma_start(gain[:, :], ln_w.partition_broadcast(P)).then_inc(ln_in, 16)
                    sp.dma_start(shift[:, :], ln_b.partition_broadcast(P)).then_inc(ln_in, 16)
            for n in range(NB):
                sp.wait_ge(norm.steps.sem, norm.steps.at(n, "shift"))
                sp.dma_start(x1_d[n * P:(n + 1) * P, :], res[:, n, :]).then_inc(stored, 16)
            sp.wait_ge(stored, 16 * NB)

        @block.tensor
        def _(pe):
            for g in range(G):
                pe.wait_ge(w_in[g % 2], 16 * (g // 2 + 1))
                for n in range(NB):
                    j = NB * g + n
                    if j >= 8:
                        pe.wait_ge(added, j - 7)
                    for k in range(KT):
                        mm = pe.matmul(ps[:, j % 8, :], mixed[:, k, n * P:(n + 1) * P], w[g % 2][:, k, :],
                                       start=(k == 0), stop=(k == KT - 1))
                    mm.then_inc(made, 1)
            pe.wait_ge(const, 2)
            pe.wait_ge(added, G * NB)
            for n in range(NB):
                pe.wait_ge(norm.steps.sem, norm.steps.at(n, "shift"))
                for k in range(0, KT, 4):
                    j = (n * KT + k) // 4
                    if j >= 8:
                        pe.wait_ge(kept, j - 7)
                    for i in range(4):
                        t = pe.transpose(ps[:, j % 8, i * P:(i + 1) * P], res[:, n, (k + i) * P:(k + i + 1) * P],
                                         ident[:, :])
                    t.then_inc(turned, 1)

        @block.scalar
        def _(act):
            norm.scalar(act, 0)
            for n in range(NB):
                if n + 1 < NB:
                    norm.scalar(act, n + 1)
                for k in range(0, KT, 4):
                    act.wait_ge(turned, (n * KT + k) // 4 + 1)
                    act.copy(x1t[:, k:k + 4, n * P:(n + 1) * P],
                             ps[:, ((n * KT + k) // 4) % 8, :].rearrange("p (i t) -> p i t", t=P)).then_inc(kept, 1)

        @block.vector
        def _(dve):
            dve.wait_ge(x_in, 16)
            for g in range(G):
                for n in range(NB):
                    j = NB * g + n
                    c = slice(GW * g, GW * (g + 1))
                    dve.wait_ge(made, j + 1)
                    dve.scalar_tensor_tensor(res[:, n, c], res[:, n, c], ALPHA, ps[:, j % 8, :],
                                             ALU.mult, ALU.add).then_inc(added, 1)
            dve.wait_ge(added, G * NB)
            dve.wait_ge(ln_in, 32)
            for n in range(NB):
                norm.vector(dve, n, res[:, n, :], gain[:, :], shift[:, :])


PH = 8
TOPK = 16
NKEY = 128
LEAST = -3.0e38
SEL = PH * TOPK


def route(nc, x1t, w_q, sub_keys, idx, gates):
    GW = 256
    NJ = 2 * PH
    with ExitStack() as ctx:
        def sb(name, shape, dt=F32):
            return ctx.enter_context(nc.sbuf_tensor("f_" + name, shape, dt))

        sem = semaphores(nc, ctx, "f_")
        ident = sb("ident", [P, P])
        keys = sb("keys", [P, 2, P])
        keys_t = sb("keys_t", [P, 2, NKEY])
        x2 = [sb(f"x2{p}", [P, KT, T], F32R) for p in range(2)]
        raw = [sb(f"raw{u}", [P, KT, GW]) for u in range(2)]
        w = [[sb(f"w{p}{r}", [P, KT, P], F32R) for r in range(2)] for p in range(2)]
        q = [sb(f"q{u}", [P, T]) for u in range(2)]
        s = [sb(f"s{u}", [P, NB, NKEY]) for u in range(4)]
        rest = sb("rest", [P, NB, NKEY])
        top = [sb(f"top{c}", [P, NB, TOPK]) for c in range(2)]
        top_i = sb("top_i", [P, 2, NB, TOPK], U32)
        top_f = sb("top_f", [P, 2, NB, TOPK])
        cand = [sb(f"cand{u}", [P, NB, TOPK * TOPK]) for u in range(2)]
        best = sb("best", [P, NB, PH, TOPK])
        pos = sb("pos", [P, NB, TOPK], U32)
        half = sb("half", [P, 2, NB, TOPK], U32)
        half_f = sb("half_f", [P, 2, NB, TOPK])
        iota = sb("iota", [P, TOPK], mybir.dt.int32)
        iota_f = sb("iota_f", [P, TOPK])
        match = [sb(f"match{u}", [P, NB * TOPK, TOPK]) for u in range(2)]
        found = sb("found", [P, 2, NB, TOPK])
        total = sb("total", [P, NB, PH])
        ps = ctx.enter_context(nc.psum_tensor("f_ps", [P, 8, T], F32))
        const, keys_in, keys_turned, keys_kept = sem("const"), sem("keys_in"), sem("keys_turned"), sem("keys_kept")
        x2_hi, x2_lo, w_hi, w_lo = sem("x2_hi"), sem("x2_lo"), sem("w_hi"), sem("w_lo")
        raw_in = [sem(f"raw_in{u}") for u in range(2)]
        q_made, q_kept, s_made, s_kept = sem("q_made"), sem("q_kept"), sem("s_made"), sem("s_kept")
        five = "max%d index%d rest%d again%d index_again%d "
        hd = Steps(sem("head"), 1,
                   five % ((0,) * 5) + five % ((1,) * 5) + "names cand " + five % ((2,) * 5) +
                   "shift mask float match0 match1 pick0 pick1 sum0 sum1 index")
        sm = Steps(hd.sem, hd.end(PH), "first less sum inverse gate")
        exped = sem("exped")
        block = ctx.enter_context(nc.Block())
        wv = w_q.rearrange("o (k p) (g c) -> g p (o k) c", p=P, c=GW)

        def part_of(eng, part, j):
            u = (j // 2) % 2
            eng.wait_ge(raw_in[u], 16 * (j // 4 + 1))
            if j >= 2:
                eng.wait_ge(q_made, j - 1)
            if part == "lo":
                eng.wait_ge(w_hi, j + 1)
            split(nc.scalar, nc.gpsimd, part, raw[u][:, :, (j % 2) * P:(j % 2 + 1) * P], w[0][j % 2][:, :, :],
                  w[1][j % 2][:, :, :], w_hi if part == "hi" else w_lo)

        @block.gpsimd
        def _(pool):
            c = Setup(pool, const)
            c.identity(ident)
            c.step(pool.iota(iota[:, :], pattern=[[1, TOPK]], base=0, channel_multiplier=0))
            assert c.n == 3
            for j in range(NJ):
                part_of(pool, "lo", j)

        @block.sync
        def _(sp):
            for g in range(NJ // 2):
                if g >= 2:
                    sp.wait_ge(w_lo, 2 * g - 2)
                sp.dma_start(raw[g % 2][:, :, :], wv[g]).then_inc(raw_in[g % 2], 16)
                if g == 0:
                    sp.dma_start(keys[:, :, :], sub_keys.rearrange("o c n d -> n (o c) d")).then_inc(keys_in, 16)

        @block.tensor
        def _(pe):
            pe.wait_ge(const, 2)
            pe.wait_ge(keys_in, 16)
            for c in range(2):
                t = pe.transpose(ps[:, 7, c * P:(c + 1) * P], keys[:, c, :], ident[:, :])
            t.then_inc(keys_turned, 1)

            def scores(j):
                pe.wait_ge(q_kept, j + 1)
                if j == 0:
                    pe.wait_ge(keys_kept, 1)
                if j >= 4:
                    pe.wait_ge(s_kept, j - 3)
                for n in range(NB):
                    mm = pe.matmul(ps[:, 4 + j % 4, n * P:(n + 1) * P], q[j % 2][:, n * P:(n + 1) * P],
                                   keys_t[:, j % 2, :], start=True, stop=True)
                mm.then_inc(s_made, 1)
            for j in range(NJ):
                pe.wait_ge(w_lo, j + 1)
                if j >= 4:
                    pe.wait_ge(q_kept, j - 3)
                for k in range(KT):
                    if j == 0:
                        pe.wait_ge(x2_lo, k + 1)
                    mm = product(pe, ps[:, j % 4, :], [w[p][j % 2][:, k, :] for p in range(2)],
                                 [x2[p][:, k, :] for p in range(2)], k == 0, k == KT - 1)
                mm.then_inc(q_made, 1)
                if j >= 1:
                    scores(j - 1)
            scores(NJ - 1)

        @block.scalar
        def _(act):
            for k in range(KT):
                if k == 8:
                    part_of(act, "hi", 0)
                split(nc.scalar, nc.vector, "hi", x1t[:, k, :], x2[0][:, k, :], x2[1][:, k, :], x2_hi)
            part_of(act, "hi", 1)
            act.wait_ge(keys_turned, 1)
            act.copy(keys_t[:, :, :].rearrange("p c n -> p (c n)"), ps[:, 7, 0:2 * P]).then_inc(keys_kept, 1)
            for j in range(NJ + 1):
                if j < NJ:
                    act.wait_ge(q_made, j + 1)
                    if j >= 2:
                        act.wait_ge(s_made, j - 1)
                    act.copy(q[j % 2][:, :], ps[:, j % 4, :]).then_inc(q_kept, 1)
                    if j + 2 < NJ:
                        part_of(act, "hi", j + 2)
                if j >= 1:
                    act.wait_ge(s_made, j)
                    if j >= 5:
                        act.wait_ge(hd.sem, hd.at((j - 5) // 2, f"rest{(j - 5) % 2}"))
                    act.copy(s[(j - 1) % 4][:, :, :].rearrange("p n k -> p (n k)"), ps[:, 4 + (j - 1) % 4, :])\
                       .then_inc(s_kept, 1)
            act.wait_ge(sm.sem, sm.at(0, "less"))
            flat = best[:, :, :, :].rearrange("p n h k -> p (n h k)")
            act.activation(flat, flat, ACT.Exp).then_inc(exped, 1)

        @block.vector
        def _(dve):
            dve.wait_ge(const, 3)
            dve.tensor_copy(iota_f[:, :], iota[:, :]).then_inc(hd.sem, 1)
            for k in range(KT):
                dve.wait_ge(x2_hi, k + 1)
                split(nc.scalar, nc.vector, "lo", x1t[:, k, :], x2[0][:, k, :], x2[1][:, k, :], x2_lo)

            def top16(c, which, keys_of, rest_of, out, out_i):
                def each(name, make, wait=True):
                    for n in range(NB):
                        ins = make(n)
                    (c.then if wait else c.mark)(f"{name}{which}", ins)
                each("max", lambda n: dve.max(out(n)[:, 0:8], keys_of(n)))
                each("index", lambda n: dve.max_index(out_i(n)[:, 0:8], out(n)[:, 0:8], keys_of(n)), False)
                each("rest", lambda n: dve.match_replace(rest_of(n), out(n)[:, 0:8], keys_of(n), LEAST))
                each("again", lambda n: dve.max(out(n)[:, 8:16], rest_of(n)))
                each("index_again", lambda n: dve.max_index(out_i(n)[:, 8:16], out(n)[:, 8:16], rest_of(n)))
            wide = [P, NB, TOPK, TOPK]
            for h in range(PH):
                c = Turn(dve, hd, h)
                for i in range(2):
                    j = 2 * h + i
                    dve.wait_ge(s_kept, j + 1)
                    top16(c, i, lambda n: s[j % 4][:, n, :], lambda n: rest[:, n, :], lambda n: top[i][:, n, :],
                          lambda n: top_i[:, i, n, :])
                c.mark("names", dve.tensor_copy(top_f[:, :, :, :].rearrange("p c n k -> p (c n k)"),
                                                top_i[:, :, :, :].rearrange("p c n k -> p (c n k)")))
                c.then("cand", dve.tensor_tensor(
                    cand[0][:, :, :].rearrange("p n (a b) -> p n a b", b=TOPK),
                    top[0][:, :, :].unsqueeze(3).broadcast_to(wide), top[1][:, :, :].unsqueeze(2).broadcast_to(wide),
                    ALU.add))
                top16(c, 2, lambda n: cand[0][:, n, :], lambda n: cand[1][:, n, :], lambda n: best[:, n, h, :],
                      lambda n: pos[:, n, :])
                c.mark("shift", dve.tensor_scalar(half[:, 0, :, :], pos[:, :, :], 4, None, ALU.logical_shift_right))
                c.then("mask", dve.tensor_scalar(half[:, 1, :, :], pos[:, :, :], 15, None, ALU.bitwise_and))
                c.then("float", dve.tensor_copy(half_f[:, :, :, :].rearrange("p c n k -> p (c n k)"),
                                                half[:, :, :, :].rearrange("p c n k -> p (c n k)")))
                one = [P, NB * TOPK, TOPK]
                for i in range(2):
                    c.mark(f"match{i}", dve.tensor_tensor(
                        match[i][:, :, :], half_f[:, i, :, :].rearrange("p n k -> p (n k)").unsqueeze(2)
                        .broadcast_to(one), iota_f[:, :].unsqueeze(1).broadcast_to(one), ALU.is_equal))
                dve.wait_ge(hd.sem, hd.at(h, "match1"))
                for i in range(2):
                    m4 = match[i][:, :, :].rearrange("p (n k) a -> p n k a", k=TOPK)
                    c.mark(f"pick{i}", dve.tensor_tensor(
                        m4, m4, top_f[:, i, :, :].unsqueeze(2).broadcast_to(wide), ALU.mult))
                dve.wait_ge(hd.sem, hd.at(h, "pick1"))
                for i in range(2):
                    c.mark(f"sum{i}", dve.tensor_reduce(found[:, i, :, :].rearrange("p n k -> p (n k)"),
                                                        match[i][:, :, :], AX, ALU.add))
                dve.wait_ge(hd.sem, hd.at(h, "sum1"))
                c.mark("index", dve.scalar_tensor_tensor(idx[:, :, h * TOPK:(h + 1) * TOPK], found[:, 0, :, :],
                                                         float(NKEY), found[:, 1, :, :], ALU.mult, ALU.add))
            c = Turn(dve, sm, 0)
            b3 = best[:, :, :, :].rearrange("p n h k -> p (n h) k")
            sums = total[:, :, :].rearrange("p n h -> p (n h)")
            over = [P, NB * PH, TOPK]
            c.then("first", dve.tensor_copy(sums, b3[:, :, 0]))
            c.mark("less", dve.tensor_tensor(b3, b3, sums.unsqueeze(2).broadcast_to(over), ALU.subtract))
            dve.wait_ge(exped, 1)
            c.then("sum", dve.tensor_reduce(sums, b3, AX, ALU.add))
            c.then("inverse", dve.reciprocal(sums, sums))
            c.mark("gate", dve.tensor_tensor(gates[:, :, :].rearrange("p n (h k) -> p (n h) k", k=TOPK), b3,
                                             sums.unsqueeze(2).broadcast_to(over), ALU.mult))


def experts(nc, x1_d, x1t, p_in, w_gate, w_proj, ple_d, idx, gates, expert_u, expert_v, ln_w, ln_b, out_d):
    RING = 4
    TURNS = SEL // RING
    GW, PD = 256, 256
    G, KP = D // GW, PD // P
    ITEMS = G * NB
    assert ITEMS == TURNS
    with ExitStack() as ctx:
        def sb(name, shape, dt=F32):
            return ctx.enter_context(nc.sbuf_tensor("h_" + name, shape, dt))

        sem = semaphores(nc, ctx, "h_")
        u_rows = [sb(f"u{r}", [P, D]) for r in range(RING)]
        v_rows = [sb(f"v{r}", [P, D]) for r in range(RING)]
        x1 = sb("x1", [P, D])
        ple = sb("ple", [P, D])
        y = [sb(f"y{r}", [P, D]) for r in range(2)]
        gain, shift = sb("gain", [P, D]), sb("shift", [P, D])
        idx_now = [sb(f"idx_now{r}", [P, RING], U32) for r in range(2)]
        dots = sb("dots", [P, RING])
        acts = sb("acts", [P, RING])
        ident = sb("ident", [P, P])
        pin = sb("pin", [P, NB, PD])
        pt = sb("pt", [P, KP, T])
        w = [sb(f"w{r}", [P, KT, GW]) for r in range(2)]
        wp = [sb(f"wp{r}", [P, KP, GW]) for r in range(2)]
        sg, pj, ple_out = ([sb(f"{n}{r}", [P, GW]) for r in range(2)] for n in ("sg", "pj", "ple_out"))
        ps = ctx.enter_context(nc.psum_tensor("h_ps", [P, 8, T], F32))
        norm = Norm(nc, ctx, "h", sem)
        ln_in, x_in, stored, seq, cleared = sem("ln_in"), sem("x_in"), sem("stored"), sem("seq"), sem("cleared")
        const, p_loaded, p_turned, p_kept, ple_in = (sem(n) for n in (
            "const", "p_loaded", "p_turned", "p_kept", "ple_in"))
        w_in = [sem(f"w_in{r}") for r in range(2)]
        ple_stored = [sem(f"ple_stored{r}") for r in range(2)]
        made, opened, product_done = sem("made"), sem("opened"), sem("product_done")
        u_in = [sem(f"u_in{r}") for r in range(RING)]
        v_in = [sem(f"v_in{r}") for r in range(RING)]
        idx_ready, dotted, gelu_done, act_done, added, summed = (
            sem(n) for n in ("idx_ready", "dotted", "gelu_done", "act_done", "added", "summed"))
        block = ctx.enter_context(nc.Block())
        uv_, vv_ = expert_u.rearrange("o e d -> (o e) d"), expert_v.rearrange("o e d -> (o e) d")

        @block.sync
        def _(sp):
            wv = w_gate.rearrange("o (k p) (g c) -> g p (o k) c", p=P, c=GW)
            wpv = w_proj.rearrange("o (k p) (g c) -> g p (o k) c", p=P, c=GW)
            pv = ple_d.rearrange("(n p) (g c) -> n g p c", p=P, c=GW)

            def load_w(g, r):
                a, b = (z[g] if isinstance(g, int) else z[bass.ds(g, 1)].rearrange("g p k c -> (g p) k c")
                        for z in (wv, wpv))
                sp.dma_start(w[r][:, :, :], a).then_inc(w_in[r], 16)
                sp.dma_start(wp[r][:, :, :], b).then_inc(w_in[r], 16)

            def store_ple(g, r):
                for n in range(NB):
                    sp.wait_ge(product_done, g * NB + (n + 3))
                    d = pv[n, g] if isinstance(g, int) else pv[n, bass.ds(g, 1)].rearrange("g p c -> (g p) c")
                    sp.dma_start(d, ple_out[n % 2][:, :]).then_inc(ple_stored[n % 2], 16)
            sp.dma_start(x1[:, :], x1_d[0:P, :]).then_inc(x_in, 16)
            sp.dma_start(pin[:, :, :], p_in.rearrange("o q (n p) d -> p (o q n) d", p=P)).then_inc(p_loaded, 16)
            for r in range(2):
                sp.sem_inc(ple_stored[r], 16)
                load_w(r, r)
            sp.dma_start(gain[:, :], ln_w.partition_broadcast(P)).then_inc(ln_in, 16)
            sp.dma_start(shift[:, :], ln_b.partition_broadcast(P)).then_inc(ln_in, 16)
            with sp.Fori(0, G // 2 - 1) as i:
                for r in range(2):
                    sp.wait_ge(made, i * (2 * NB) + (r + 1) * NB)
                    load_w(i * 2 + (r + 2), r)
                    store_ple(i * 2 + r, r)
            for r in range(2):
                store_ple(G - 2 + r, r)
            for r in range(2):
                sp.wait_ge(ple_stored[r], 16 * ITEMS // 2 + 16)
            for n in range(NB):
                if n >= 1:
                    sp.wait_ge(summed, 4 * n)
                    sp.dma_start(x1[:, :], x1_d[n * P:(n + 1) * P, :]).then_inc(x_in, 16)
                sp.dma_start(ple[:, :], ple_d[n * P:(n + 1) * P, :]).then_inc(ple_in, 16)
                sp.wait_ge(norm.steps.sem, norm.steps.at(n, "shift"))
                sp.dma_start(out_d[0, n * P:(n + 1) * P, :], y[0][:, :]).then_inc(stored, 16)
            sp.wait_ge(stored, 16 * NB)

        @block.tensor
        def _(pe):
            pe.sem_inc(opened, 8)
            pe.wait_ge(const, 2)
            pe.wait_ge(p_loaded, 16)
            for k in range(KP):
                for n in range(NB):
                    t = pe.transpose(ps[:, k, n * P:(n + 1) * P], pin[:, n, k * P:(k + 1) * P], ident[:, :])
                t.then_inc(p_turned, 1)
            pe.wait_ge(p_kept, KP)
            with pe.Fori(0, G // 2) as i:
                for r in range(2):
                    pe.wait_ge(w_in[r], i * 32 + 32)
                    for n in range(NB):
                        bank = NB * r + n
                        pe.wait_ge(opened, i * (2 * NB) + (bank + 1))
                        for k in range(KT):
                            pe.matmul(ps[:, bank, 0:GW], x1t[:, k, n * P:(n + 1) * P], w[r][:, k, :],
                                      start=(k == 0), stop=(k == KT - 1))
                        for k in range(KP):
                            mm = pe.matmul(ps[:, bank, GW:2 * GW], pt[:, k, n * P:(n + 1) * P], wp[r][:, k, :],
                                           start=(k == 0), stop=(k == KP - 1))
                        mm.then_inc(made, 1)

        @block.gpsimd
        def _(pool):
            Setup(pool, const).identity(ident)
            pool.sem_inc(product_done, 2)
            for n in range(NB):
                with pool.Fori(0, TURNS // 2) as i:
                    for b in range(2):
                        t = i * 2 + (n * TURNS + b)
                        pool.wait_ge(idx_ready, t + 1)
                        pool.sem_inc(seq, 1)
                        for ready, rows, table, slots in ((dotted, u_rows, uv_, u_in), (added, v_rows, vv_, v_in)):
                            for r in range(RING):
                                pool.wait_ge(ready, t * RING + (r + 2))
                                pool.sem_inc(seq, 1)
                                pool.indirect_dma_start(
                                    rows[r][:, :], None, table,
                                    bass.IndirectOffsetOnAxis(ap=idx_now[b][:, r:r + 1], axis=0)).then_inc(slots[r], 16)
                        if n == 0:
                            pool.wait_ge(ple_stored[b], i * 16 + 16)
                            pool.wait_ge(opened, i * 2 + (b + 9))
                            pool.tensor_tensor(ple_out[b][:, :], sg[b][:, :], pj[b][:, :], ALU.mult)\
                                .then_inc(product_done, 1)

        @block.scalar
        def _(act):
            for k in range(KP):
                act.wait_ge(p_turned, k + 1)
                act.copy(pt[:, k, :], ps[:, k, :]).then_inc(p_kept, 1)

            def factors(t, bank):
                act.wait_ge(made, t + 1)
                act.wait_ge(product_done, t + 1)
                act.activation(sg[bank % 2][:, :], ps[:, bank, 0:GW], ACT.Sigmoid)
                act.copy(pj[bank % 2][:, :], ps[:, bank, GW:2 * GW]).then_inc(opened, 1)
            for n in range(NB):
                per = 8 if n == 0 else 2
                with act.Fori(0, TURNS // per) as i:
                    for j in range(per):
                        b = j % 2
                        t = i * per + (n * TURNS + j)
                        act.wait_ge(added, t * RING + 1)
                        act.copy(idx_now[b][:, :], idx[:, n, bass.ds(i * (per * RING) + j * RING, RING)])\
                           .then_inc(idx_ready, 1)
                        act.wait_ge(dotted, (t + 2) * RING + 1)
                        act.activation(acts[:, :], dots[:, :], ACT.Gelu).then_inc(gelu_done, 1)
                        if n == 0:
                            factors(t, j)
                norm.scalar(act, n)

        @block.vector
        def _(dve):
            dve.sem_inc(dotted, RING + 1)
            dve.sem_inc(added, RING + 1)
            dve.sem_inc(act_done, 1)
            for n in range(NB):
                if n >= 1:
                    dve.wait_ge(stored, 16 * n)
                for r in range(2):
                    dve.memset(y[r][:, :], 0.0).then_inc(cleared, 1)
                dve.wait_ge(x_in, 16 * (n + 1))
                dve.wait_ge(cleared, 2 * (n + 1))
                with dve.Fori(0, TURNS) as i:
                    t = i + n * TURNS
                    for r in range(RING):
                        dve.wait_ge(u_in[r], t * 16 + 16)
                        if r == 0:
                            dve.wait_ge(act_done, t + 1)
                        dve.tensor_tensor_reduce(u_rows[r][:, :], u_rows[r][:, :], x1[:, :], 1.0, 0.0, ALU.mult, ALU.add,
                                                 dots[:, r:r + 1]).then_inc(dotted, 1)
                    dve.wait_ge(gelu_done, t + 1)
                    dve.tensor_tensor(acts[:, :], acts[:, :], gates[:, n, bass.ds(i * RING, RING)], ALU.mult)\
                       .then_inc(act_done, 1)
                    dve.wait_ge(act_done, t + 2)
                    for r in range(RING):
                        dve.wait_ge(v_in[r], t * 16 + 16)
                        dve.wait_ge(added, t * RING + (r + RING))
                        dve.scalar_tensor_tensor(y[r % 2][:, :], v_rows[r][:, :], acts[:, r:r + 1], y[r % 2][:, :],
                                                 ALU.mult, ALU.add).then_inc(added, 1)
                dve.wait_ge(added, RING * (TURNS * (n + 1) + 1) + 1)
                dve.tensor_tensor(y[0][:, :], y[0][:, :], y[1][:, :], ALU.add).then_inc(summed, 1)
                dve.wait_ge(summed, 4 * n + 1)
                dve.scalar_tensor_tensor(y[0][:, :], x1[:, :], ALPHA, y[0][:, :], ALU.mult, ALU.add)\
                   .then_inc(summed, 1)
                dve.wait_ge(summed, 4 * n + 2)
                dve.wait_ge(ple_in, 16 * (n + 1))
                dve.tensor_tensor(y[0][:, :], y[0][:, :], ple[:, :], ALU.add).then_inc(summed, 2)
                dve.wait_ge(summed, 4 * n + 4)
                if n == 0:
                    dve.wait_ge(ln_in, 32)
                norm.vector(dve, n, y[0][:, :], gain[:, :], shift[:, :])


def build(nc, a, out):
    def dram(name, shape):
        return nc.dram_tensor(name, shape, F32, kind="Internal").ap()
    proj_t = dram("proj_t", [IN_COLS, T])
    ar_d, bk_t_d = dram("ar_d", [NC, P, MB, 2 * L]), dram("bk_t_d", [NC, P, MB, P])
    g_d, v_d = dram("g_d", [NC, P, H, 2 * L]), dram("v_d", [NC, L, MB, P])
    bonus_d, gate_d = dram("bonus_d", [MB, P, T]), dram("gate_d", [MB, P, T])
    cols_d, decay_d = dram("cols_d", [P, 6 + len(PARAMS), MB]), dram("decay_d", [P, MB, NC])
    wt_d, y_d, at_d = dram("wt_d", [NC, L, H, L]), dram("y_d", [T, W]), dram("at_d", [MB, P, T])
    x1_d, ple_d = dram("x1_d", [T, D]), dram("ple_d", [T, D])
    vecs = [a[n].rearrange("o (m e) j -> (o m) (e j)", e=2) if n == "rwkv_r_k" else
            a[n].rearrange("o (m p) -> (o m) p", p=P) for n in PARAMS]

    project_in(nc, a["x"], a["w_in"], proj_t)
    rwkv_prepare(nc, proj_t, a["rwkv_mu"], vecs, a["rwkv_w_lora1"], a["rwkv_w_lora2"], a["rwkv_a_lora1"],
                 a["rwkv_a_lora2"], a["rwkv_g_lora1"], a["rwkv_g_lora2"],
                 ar_d, bk_t_d, g_d, v_d, bonus_d, gate_d, cols_d, decay_d)
    attention_and_inverse(nc, proj_t, at_d, g_d, wt_d)
    rwkv_scan(nc, ar_d, bk_t_d, g_d, v_d, decay_d, wt_d, y_d)
    with ExitStack() as ctx:
        idx = ctx.enter_context(nc.sbuf_tensor("idx", [P, NB, SEL], U32))
        gates = ctx.enter_context(nc.sbuf_tensor("gates", [P, NB, SEL], F32))
        with nc.sbuf_tensor("x1t", [P, KT, T], F32) as x1t:
            with nc.sbuf_tensor("mixed", [P, KT, T], F32) as mixed:
                with nc.sbuf_tensor("yb", [P, MB, T], F32) as yb:
                    rwkv_finish(nc, y_d, cols_d, bonus_d, gate_d, yb)
                    mix(nc, proj_t, at_d, yb, a["w_up_a"], a["w_up_b"], mixed)
                out_project(nc, mixed, a["w_o"], a["x"], a["ln1_w"], a["ln1_b"], x1_d, x1t)
            route(nc, x1t, a["peer_w_q"], a["peer_sub_keys"], idx, gates)
            experts(nc, x1_d, x1t, a["p"], a["ple_w_gate"], a["ple_w_proj"], ple_d, idx, gates, a["peer_u"], a["peer_v"],
                    a["ln2_w"], a["ln2_b"], out)


INPUTS = ["x", "p", "w_in", "rwkv_mu", "rwkv_w0", "rwkv_w_lora1", "rwkv_w_lora2", "rwkv_a0", "rwkv_a_lora1",
          "rwkv_a_lora2", "rwkv_g_lora1", "rwkv_g_lora2", "rwkv_k_k", "rwkv_k_a", "rwkv_r_k", "rwkv_lnx_w",
          "rwkv_lnx_b", "w_up_a", "w_up_b", "w_o", "ln1_w", "ln1_b", "peer_w_q", "peer_sub_keys", "peer_u",
          "peer_v", "ple_w_gate", "ple_w_proj", "ln2_w", "ln2_b"]


def kernel(**inputs):
    import numpy as np
    import concourse.bacc as bacc
    from concourse.bass_utils import run_bass_kernel_spmd

    nc = bacc.Bacc("TRN2", target_bir_lowering=False, num_devices=1)
    arrays, a = {}, {}
    for name in INPUTS:
        arrays[f"in_{name}"] = np.ascontiguousarray(inputs[name])
        a[name] = nc.dram_tensor(f"in_{name}", arrays[f"in_{name}"].shape, F32, kind="ExternalInput").ap()
    out = nc.dram_tensor("out", (1, T, D), F32, kind="ExternalOutput").ap()
    build(nc, a, out)
    return run_bass_kernel_spmd(nc, [arrays], core_ids=[0]).results[0]["out"]
```
